# Optimizing a Trainium2 kernel written in Bass

```python
import math
import jax, jax.numpy as jnp
from jax import lax
import numpy as np

D_MODEL = 1024
BATCH = 1
SEQ = 512
DEPTH = 2

N_META = 16
MLA_HEADS = 8
MLA_Q_RANK = 256
MLA_KV_RANK = 128
MLA_NOPE = 64
MLA_ROPE = 32
MLA_V = 64
ROPE_THETA = 10000.0
ATT_BLOCK = 128
DN_HEADS = 4
DN_DK = 128
DN_DV = 128
DN_CONV = 4
DN_CHUNK = 64
CV_CH = 512
CV_WIDTH = 31
D_FF = 2816
N_EXPERTS = 8
TOP_K = 2
D_FF_EXPERT = 1408
ALPHA = (2 * DEPTH) ** 0.25
BETA = (8 * DEPTH) ** -0.25
EPS = 1e-6
NEG_INF = -1e30

MLA_QK = MLA_NOPE + MLA_ROPE
DN_QKV = 2 * DN_HEADS * DN_DK + DN_HEADS * DN_DV
IN_SIZES = (MLA_Q_RANK, MLA_KV_RANK, MLA_ROPE, DN_QKV, DN_HEADS * DN_DV, DN_HEADS, DN_HEADS, CV_CH, CV_CH, D_MODEL, D_MODEL, D_MODEL)
IN_COLS = sum(IN_SIZES)

kernel_name = 'hybrid_gated_mla_deltanet_conformer_moe'

def _split(t, sizes):
    return jnp.split(t, np.cumsum(sizes)[:-1].tolist(), axis=-1)

def _pad_front(t, n):
    return jnp.pad(t, [(0, 0), (n, 0)] + [(0, 0)] * (t.ndim - 2))

def layer_norm(x, g, b):
    xf = x.astype(jnp.float32)
    mu = jnp.mean(xf, -1, keepdims=True)
    var = jnp.mean(jnp.square(xf - mu), -1, keepdims=True)
    return ((xf - mu) * lax.rsqrt(var + EPS) * g.astype(jnp.float32) + b.astype(jnp.float32)).astype(x.dtype)

def rms_norm(x, g):
    xf = x.astype(jnp.float32)
    return (xf * lax.rsqrt(jnp.mean(jnp.square(xf), -1, keepdims=True) + EPS) * g.astype(jnp.float32)).astype(x.dtype)

def l2_norm(x):
    xf = x.astype(jnp.float32)
    return xf * lax.rsqrt(jnp.sum(jnp.square(xf), -1, keepdims=True) + EPS)

def rope_tables(n_pos, dim):
    inv_freq = ROPE_THETA ** (-jnp.arange(0, dim, 2, dtype=jnp.float32) / dim)
    ang = jnp.arange(n_pos, dtype=jnp.float32)[:, None] * inv_freq[None, :]
    return jnp.cos(ang), jnp.sin(ang)

def apply_rope(x, cos, sin):
    x1, x2 = jnp.split(x.astype(jnp.float32), 2, axis=-1)
    return jnp.concatenate([x1 * cos - x2 * sin, x2 * cos + x1 * sin], -1).astype(x.dtype)

def causal_dwconv(x, w):
    width, ch = w.shape
    return lax.conv_general_dilated(x, w[:, None, :].astype(x.dtype), window_strides=(1,), padding=[(width - 1, 0)], dimension_numbers=('NWC', 'WIO', 'NWC'), feature_group_count=ch)

def mla_branch(c_q, c_kv, k_r, q_norm, w_uq, kv_norm, w_ukv, cos, sin):
    B, L, _ = c_q.shape
    q = (rms_norm(c_q, q_norm) @ w_uq).reshape(B, L, MLA_HEADS, MLA_QK)
    q_nope = q[..., :MLA_NOPE]
    q_rope = apply_rope(q[..., MLA_NOPE:], cos[:, None, :], sin[:, None, :])
    kv = (rms_norm(c_kv, kv_norm) @ w_ukv).reshape(B, L, MLA_HEADS, MLA_NOPE + MLA_V)
    k_nope, v = kv[..., :MLA_NOPE], kv[..., MLA_NOPE:]
    k_rope = apply_rope(k_r, cos, sin)
    pad = ATT_BLOCK - N_META
    q_nope, q_rope, k_nope, k_rope, v = (_pad_front(t, pad) for t in (q_nope, q_rope, k_nope, k_rope, v))
    Lp = L + pad
    n_blocks = Lp // ATT_BLOCK
    scale = MLA_QK ** -0.5
    key_pos = jnp.arange(Lp)

    def one_block(i):
        start = i * ATT_BLOCK
        qn = lax.dynamic_slice_in_dim(q_nope, start, ATT_BLOCK, axis=1)
        qr = lax.dynamic_slice_in_dim(q_rope, start, ATT_BLOCK, axis=1)
        s = jnp.einsum('bqhd,bkhd->bhqk', qn, k_nope) + jnp.einsum('bqhd,bkd->bhqk', qr, k_rope)
        s = s.astype(jnp.float32) * scale
        q_pos = start + jnp.arange(ATT_BLOCK)
        mask = (key_pos[None, :] <= q_pos[:, None]) & (key_pos[None, :] >= pad)
        p = jax.nn.softmax(jnp.where(mask, s, NEG_INF), axis=-1).astype(v.dtype)
        return jnp.einsum('bhqk,bkhd->bqhd', p, v)

    o = lax.map(one_block, jnp.arange(n_blocks))
    o = jnp.transpose(o, (1, 0, 2, 3, 4)).reshape(B, Lp, MLA_HEADS * MLA_V)
    return o[:, pad:]

def gated_deltanet_branch(qkv, z, b_logit, a_logit, conv_w, a_log, dt_bias, o_norm):
    B, L, _ = qkv.shape
    dtype = qkv.dtype
    qkv = jax.nn.silu(causal_dwconv(qkv, conv_w))
    q, k, v = _split(qkv, (DN_HEADS * DN_DK, DN_HEADS * DN_DK, DN_HEADS * DN_DV))
    q = l2_norm(q.reshape(B, L, DN_HEADS, DN_DK)) * (DN_DK ** -0.5)
    k = l2_norm(k.reshape(B, L, DN_HEADS, DN_DK))
    v = v.reshape(B, L, DN_HEADS, DN_DV).astype(jnp.float32)
    beta = jax.nn.sigmoid(b_logit.astype(jnp.float32))
    g = -jnp.exp(a_log.astype(jnp.float32)) * jax.nn.softplus(a_logit.astype(jnp.float32) + dt_bias.astype(jnp.float32))
    pad = DN_CHUNK - N_META
    q, k, v, beta, g = (_pad_front(t, pad) for t in (q, k, v, beta, g))
    Lp = L + pad
    n_chunks = Lp // DN_CHUNK

    def to_chunks(t):
        t = t.reshape((B, n_chunks, DN_CHUNK) + t.shape[2:])
        return jnp.moveaxis(t, 3, 1)

    qc, kc, vc, bc = to_chunks(q), to_chunks(k), to_chunks(v), to_chunks(beta)
    gc = jnp.cumsum(to_chunks(g), axis=-1)
    incl = jnp.tril(jnp.ones((DN_CHUNK, DN_CHUNK), dtype=bool))
    strict = jnp.tril(jnp.ones((DN_CHUNK, DN_CHUNK), dtype=bool), k=-1)
    gamma = jnp.exp(jnp.where(incl, gc[..., :, None] - gc[..., None, :], -jnp.inf))
    kb = kc * bc[..., None]
    a_mat = jnp.where(strict, jnp.einsum('bhnid,bhnjd->bhnij', kb, kc) * gamma, 0.0)
    eye = jnp.eye(DN_CHUNK, dtype=jnp.float32)
    rhs = jnp.concatenate([vc * bc[..., None], kb * jnp.exp(gc)[..., None]], axis=-1)
    sol = lax.linalg.triangular_solve(a_mat + eye, rhs, left_side=True, lower=True, unit_diagonal=True)
    u_base, w_dec = sol[..., :DN_DV], sol[..., DN_DV:]
    qk = jnp.einsum('bhnid,bhnjd->bhnij', qc, kc) * gamma
    q_dec = qc * jnp.exp(gc)[..., None]
    k_dec = kc * jnp.exp(gc[..., -1:] - gc)[..., None]
    chunk_decay = jnp.exp(gc[..., -1])

    def step(state, xs):
        u_b, w_i, qk_i, qd_i, kd_i, cd_i = xs
        u = u_b - jnp.einsum('bhcd,bhde->bhce', w_i, state)
        o = jnp.einsum('bhcd,bhde->bhce', qd_i, state) + jnp.einsum('bhij,bhje->bhie', qk_i, u)
        state = state * cd_i[..., None, None] + jnp.einsum('bhcd,bhce->bhde', kd_i, u)
        return state, o

    xs = tuple(jnp.moveaxis(t, 2, 0) for t in (u_base, w_dec, qk, q_dec, k_dec, chunk_decay))
    s0 = jnp.zeros((B, DN_HEADS, DN_DK, DN_DV), jnp.float32)
    _, o = lax.scan(step, s0, xs)
    o = jnp.transpose(o, (1, 0, 3, 2, 4)).reshape(B, Lp, DN_HEADS, DN_DV)[:, pad:]
    o = rms_norm(o, o_norm) * jax.nn.silu(z.reshape(B, L, DN_HEADS, DN_DV).astype(jnp.float32))
    return o.reshape(B, L, DN_HEADS * DN_DV).astype(dtype)

def conformer_conv_branch(a, b, dw_w, dw_b, ln_g, ln_b):
    h = a * jax.nn.sigmoid(b)
    h = causal_dwconv(h, dw_w) + dw_b
    return jax.nn.silu(layer_norm(h, ln_g, ln_b))

def mixer(h, w_in, q_norm, w_uq, kv_norm, w_ukv, dn_conv_w, dn_a_log, dn_dt_bias, dn_o_norm, cv_dw_w, cv_dw_b, cv_ln_g, cv_ln_b, w_br_mla, w_br_dn, w_br_cv, w_mix_out, cos, sin):
    proj = h @ w_in
    c_q, c_kv, k_r, dn_qkv, dn_z, dn_b, dn_a, cv_a, cv_b, g_mla, g_dn, g_cv = _split(proj, IN_SIZES)
    y_mla = mla_branch(c_q, c_kv, k_r, q_norm, w_uq, kv_norm, w_ukv, cos, sin) @ w_br_mla
    y_dn = gated_deltanet_branch(dn_qkv, dn_z, dn_b, dn_a, dn_conv_w, dn_a_log, dn_dt_bias, dn_o_norm) @ w_br_dn
    y_cv = conformer_conv_branch(cv_a, cv_b, cv_dw_w, cv_dw_b, cv_ln_g, cv_ln_b) @ w_br_cv
    merged = jax.nn.sigmoid(g_mla) * y_mla + jax.nn.sigmoid(g_dn) * y_dn + jax.nn.sigmoid(g_cv) * y_cv
    return merged @ w_mix_out

def swiglu(x, w_gate, w_up, w_down):
    return (jax.nn.silu(x @ w_gate) * (x @ w_up)) @ w_down

def moe_swiglu(x, w_router, w_gate, w_up, w_down):
    B, L, D = x.shape
    xt = x.reshape(B * L, D)
    logits = (xt @ w_router).astype(jnp.float32)
    top_v, top_i = lax.top_k(logits, TOP_K)
    top_w = jax.nn.softmax(top_v, axis=-1)
    gates = jnp.sum(jax.nn.one_hot(top_i, N_EXPERTS, dtype=jnp.float32) * top_w[..., None], axis=1).astype(x.dtype)
    y = jnp.zeros_like(xt)
    for e in range(N_EXPERTS):
        y = y + gates[:, e:e + 1] * swiglu(xt, w_gate[e], w_up[e], w_down[e])
    return y.reshape(B, L, D)

def setup_inputs(seed: int = 0) -> dict:
    key = jax.random.key(seed)
    keys = iter(jax.random.split(key, 48))
    n_dense = (DEPTH + 1) // 2
    n_moe = DEPTH // 2

    def nrm(shape, scale):
        return jax.random.normal(next(keys), shape, jnp.float32) * scale

    dt = jnp.exp(jax.random.uniform(next(keys), (DEPTH, DN_HEADS), jnp.float32, minval=math.log(1e-3), maxval=math.log(1e-1)))
    return {
        'x': nrm((BATCH, SEQ, D_MODEL), 1.0),
        'meta_tokens': nrm((N_META, D_MODEL), 1.0),
        'w_in': nrm((DEPTH, D_MODEL, IN_COLS), D_MODEL ** -0.5),
        'mla_q_norm': 1.0 + nrm((DEPTH, MLA_Q_RANK), 0.02),
        'mla_w_uq': nrm((DEPTH, MLA_Q_RANK, MLA_HEADS * MLA_QK), MLA_Q_RANK ** -0.5),
        'mla_kv_norm': 1.0 + nrm((DEPTH, MLA_KV_RANK), 0.02),
        'mla_w_ukv': nrm((DEPTH, MLA_KV_RANK, MLA_HEADS * (MLA_NOPE + MLA_V)), MLA_KV_RANK ** -0.5),
        'dn_conv_w': nrm((DEPTH, DN_CONV, DN_QKV), DN_CONV ** -0.5),
        'dn_a_log': jnp.log(jax.random.uniform(next(keys), (DEPTH, DN_HEADS), jnp.float32, minval=1.0, maxval=16.0)),
        'dn_dt_bias': dt + jnp.log(-jnp.expm1(-dt)),
        'dn_o_norm': 1.0 + nrm((DEPTH, DN_DV), 0.02),
        'cv_dw_w': nrm((DEPTH, CV_WIDTH, CV_CH), CV_WIDTH ** -0.5),
        'cv_dw_b': nrm((DEPTH, CV_CH), 0.01),
        'cv_ln_g': 1.0 + nrm((DEPTH, CV_CH), 0.02),
        'cv_ln_b': nrm((DEPTH, CV_CH), 0.01),
        'w_br_mla': nrm((DEPTH, MLA_HEADS * MLA_V, D_MODEL), (MLA_HEADS * MLA_V) ** -0.5 * BETA),
        'w_br_dn': nrm((DEPTH, DN_HEADS * DN_DV, D_MODEL), (DN_HEADS * DN_DV) ** -0.5 * BETA),
        'w_br_cv': nrm((DEPTH, CV_CH, D_MODEL), CV_CH ** -0.5 * BETA),
        'w_mix_out': nrm((DEPTH, D_MODEL, D_MODEL), D_MODEL ** -0.5 * BETA),
        'ln1_g': 1.0 + nrm((DEPTH, D_MODEL), 0.02),
        'ln1_b': nrm((DEPTH, D_MODEL), 0.01),
        'ln2_g': 1.0 + nrm((DEPTH, D_MODEL), 0.02),
        'ln2_b': nrm((DEPTH, D_MODEL), 0.01),
        'ffn_w_gate': nrm((n_dense, D_MODEL, D_FF), D_MODEL ** -0.5),
        'ffn_w_up': nrm((n_dense, D_MODEL, D_FF), D_MODEL ** -0.5),
        'ffn_w_down': nrm((n_dense, D_FF, D_MODEL), D_FF ** -0.5 * BETA),
        'moe_w_router': nrm((n_moe, D_MODEL, N_EXPERTS), D_MODEL ** -0.5),
        'moe_w_gate': nrm((n_moe, N_EXPERTS, D_MODEL, D_FF_EXPERT), D_MODEL ** -0.5),
        'moe_w_up': nrm((n_moe, N_EXPERTS, D_MODEL, D_FF_EXPERT), D_MODEL ** -0.5),
        'moe_w_down': nrm((n_moe, N_EXPERTS, D_FF_EXPERT, D_MODEL), D_FF_EXPERT ** -0.5 * BETA),
    }

def reference(x, meta_tokens, w_in, mla_q_norm, mla_w_uq, mla_kv_norm, mla_w_ukv, dn_conv_w, dn_a_log, dn_dt_bias, dn_o_norm, cv_dw_w, cv_dw_b, cv_ln_g, cv_ln_b, w_br_mla, w_br_dn, w_br_cv, w_mix_out, ln1_g, ln1_b, ln2_g, ln2_b, ffn_w_gate, ffn_w_up, ffn_w_down, moe_w_router, moe_w_gate, moe_w_up, moe_w_down):
    B = x.shape[0]
    meta = jnp.broadcast_to(meta_tokens[None].astype(x.dtype), (B, N_META, D_MODEL))
    h = jnp.concatenate([meta, x], axis=1)
    cos, sin = rope_tables(h.shape[1], MLA_ROPE)
    for l in range(DEPTH):
        mix = mixer(h, w_in[l], mla_q_norm[l], mla_w_uq[l], mla_kv_norm[l], mla_w_ukv[l], dn_conv_w[l], dn_a_log[l], dn_dt_bias[l], dn_o_norm[l], cv_dw_w[l], cv_dw_b[l], cv_ln_g[l], cv_ln_b[l], w_br_mla[l], w_br_dn[l], w_br_cv[l], w_mix_out[l], cos, sin)
        h = layer_norm(ALPHA * h + mix, ln1_g[l], ln1_b[l])
        if l % 2 == 0:
            f = swiglu(h, ffn_w_gate[l // 2], ffn_w_up[l // 2], ffn_w_down[l // 2])
        else:
            f = moe_swiglu(h, moe_w_router[l // 2], moe_w_gate[l // 2], moe_w_up[l // 2], moe_w_down[l // 2])
        h = layer_norm(ALPHA * h + f, ln2_g[l], ln2_b[l])
    return h[:, N_META:]


_drawn_inputs = setup_inputs


def setup_inputs(seed=0):
    import zlib

    import numpy as np

    out = dict(_drawn_inputs(seed))
    spreads = {}
    factors = {'mla_q_norm': 8.0,
     'mla_kv_norm': 8.0,
     'dn_a_log': 2.798,
     'dn_o_norm': 8.0,
     'cv_dw_b': 7.789,
     'cv_ln_g': 5.684,
     'cv_ln_b': 8.0,
     'ln1_b': 2.831,
     'ln2_b': 3.2}
    for name, (base, spread) in spreads.items():
        noise = np.random.default_rng([zlib.crc32(name.encode()), seed]).standard_normal(out[name].shape)
        drawn = base * np.exp(spread * noise) if base else spread * noise
        out[name] = __import__('jax').numpy.asarray(drawn.astype(out[name].dtype))
    for name, factor in factors.items():
        out[name] = (out[name] * factor).astype(out[name].dtype)
    return out
```

```python
from contextlib import ExitStack

import numpy as np

import concourse.bass as bass
import concourse.mybir as mybir
from concourse.alu_op_type import AluOpType as ALU

F32 = mybir.dt.float32
F32R = mybir.dt.float32r
U32 = mybir.dt.uint32
ACT = mybir.ActivationFunctionType
AX = mybir.AxisListType.X

P = 128
D = 1024
KD = D // P
N_META, SEQ = 16, 512
T = N_META + SEQ
HALF = T // 2
DEPTH = 2
HEADS, NOPE, ROPE, VD = 8, 64, 32, 64
QK = NOPE + ROPE
DN_H = 4
CV_W = 31
ALPHA = (2 * DEPTH) ** 0.25
EPS = 1e-6
NEG = -1e30
N_EXP = 8
F_TILES = 11
TILES = [(0, N_META)] + [(N_META + P * i, P) for i in range(SEQ // P)]
NT = len(TILES)
WIN = [s for s, _ in TILES]
LEVELS = 7

MIX_PANELS = 76
MIX_TILES = 102
RAW = 4
WIDE, DEEP = KD * P, F_TILES * P
EXPERTS = (2, N_EXP)
PER_EXPERT = 2 * F_TILES + KD

SEGMENTS = [("qkv", 12), ("ba", 1), ("z", 4), ("br0", 16), ("c", 4), ("uq", 8), ("kn", 4), ("v", NT),
            ("br1", 16), ("cv", 8), ("br2", 16), ("mix", 8)]
TILE0, _n = {}, 0
for _name, _k in SEGMENTS:
    TILE0[_name] = _n
    _n += _k
assert _n == MIX_TILES
LAST_TILE = ([TILE0["qkv"] + i for i in range(12)] + [TILE0["ba"]] + [TILE0["z"] + i for i in range(4)]
             + [TILE0["br0"] + 4 * i + j for i in range(4) for j in (0, 2, 3)]
             + [TILE0["c"] + i for i in range(4)] + [TILE0["uq"] + 3, TILE0["uq"] + 7]
             + [TILE0["v"] + NT - 1]
             + [TILE0["br1"] + 4 * i + j for i in range(4) for j in (0, 2, 3)]
             + [TILE0["cv"] + i for i in range(8)]
             + [TILE0["br2"] + 4 * i + j for i in range(4) for j in (0, 2, 3)]
             + [TILE0["mix"] + i for i in range(8)])
assert len(LAST_TILE) == MIX_PANELS

VEC = {}
_n = 0
for _name, _k in (("q_norm", 2), ("kv_norm", 1), ("conv", 12 * 4), ("o_norm", 1), ("cvw", 4 * CV_W), ("cvb", 4),
                  ("cvg", 4), ("cvlb", 4), ("ln1g", 8), ("ln1b", 8), ("ln2g", 8), ("ln2b", 8),
                  ("a_log", 4), ("dt", 4)):
    VEC[_name] = _n
    _n += _k
NVEC = _n


class Counts:

    def __init__(self, notes=None):
        self.first = notes is None
        self.notes = {} if notes is None else notes
        self.raised = {}
        self.sems = {}

    def mark(self, name, label, n=1):
        self.raised[name] = self.raised.get(name, 0) + n
        if self.first:
            assert label not in self.notes, label
            self.notes[label] = (name, self.raised[name])
        return self.sems[name], n

    def at(self, label):
        if self.first and label not in self.notes:
            return next(iter(self.sems.values())), 1
        name, value = self.notes[label]
        return self.sems[name], value


def program(nc, counts, ins, out):
    mark, at = counts.mark, counts.at
    with ExitStack() as ctx:
        _program(nc, ctx, counts, mark, at, ins, out)


def _program(nc, ctx, counts, mark, at, ins, out):
    def sb(name, shape, dt=F32, where=None):
        return (where or ctx).enter_context(nc.sbuf_tensor(name, shape, dt))

    def sem(name):
        s = ctx.enter_context(nc.semaphore(name))
        counts.sems[name] = s
        return s

    h_hi = sb("h_hi", [P, KD, T], F32R)
    h_lo = sb("h_lo", [P, KD, T], F32R)
    raw = sb("raw", [P, RAW, DEEP])
    w_hi = sb("w_hi", [P, 2, DEEP], F32R)
    w_lo = sb("w_lo", [P, 2, DEEP], F32R)
    ident = sb("ident", [P, P])
    ones = sb("ones", [P, P])
    cum_mask = sb("cum_mask", [P, P])
    neg_ji = sb("neg_ji", [P, P])
    neg_qk = sb("neg_qk", [P, P])
    level_mask = sb("level_mask", [P, LEVELS, P])
    meta_rows = sb("meta_rows", [P, NT, DN_H])
    rope = sb("rope", [P, T])
    expert_no = sb("expert_no", [P, N_EXP])
    eps = sb("eps", [P, 1])
    vec = sb("vec", [P, NVEC])
    router = sb("router", [P, KD, N_EXP])
    router_hi = sb("router_hi", [P, KD, N_EXP], F32R)
    router_lo = sb("router_lo", [P, KD, N_EXP], F32R)
    acc = sb("acc", [P, KD, T])
    br_hi = sb("br_hi", [P, 4, T], F32R)
    br_lo = sb("br_lo", [P, 4, T], F32R)
    gate_s = sb("gate_s", [P, 2, T])
    tmp_s = sb("tmp_s", [P, 2, T])

    ph = ExitStack()
    qkv = sb("qkv", [P, 12, T], where=ph)
    ba = sb("ba", [P, NT, 8], where=ph)
    g_tok = sb("g_tok", [P, NT, DN_H], where=ph)
    b_tok = sb("b_tok", [P, NT, DN_H], where=ph)
    sp1 = sb("sp1", [P, NT, DN_H], where=ph)
    sp2 = sb("sp2", [P, NT, DN_H], where=ph)
    ea = sb("ea", [P, DN_H], where=ph)
    cums = sb("cums", [P, NT, 2 * DN_H], where=ph)
    ecum = sb("ecum", [P, NT, 2 * DN_H], where=ph)
    eneg = sb("eneg", [P, NT, DN_H], where=ph)
    conv_ph = ExitStack()
    x_pad = sb("x_pad", [P, 2, 3 + T], where=conv_ph)
    conv_o = sb("conv_o", [P, 2, T], where=conv_ph)
    conv_ph.close()
    GRP = 3
    wk = sb("wk", [P, 2, 4, P], where=ph)
    dT = sb("dT", [P, GRP, 4, P], where=ph)
    dN = sb("dN", [P, GRP, 4, P], where=ph)
    aN = sb("aN", [P, GRP, 4, P], where=ph)
    lvl_e = sb("lvl_e", [P, 3, 4, P], where=ph)
    lvl_x = sb("lvl_x", [P, 3, 4, P], where=ph)
    qkg = sb("qkg", [P, GRP, 4, P], where=ph)
    kdec = sb("kdec", [P, GRP, 4, P], where=ph)
    vtok = sb("vtok", [P, GRP, 4, P], where=ph)
    state = sb("state", [P, 4, P], where=ph)
    ph.close()
    ph = ExitStack()
    c_f = sb("c_f", [P, 3, T], where=ph)
    cn_hi = sb("cn_hi", [P, 3, T], F32R, where=ph)
    cn_lo = sb("cn_lo", [P, 3, T], F32R, where=ph)
    qT = sb("qT", [P, HEADS, T], where=ph)
    kT = sb("kT", [P, HEADS, T], where=ph)
    v_tok = sb("v_tok", [P, NT, HEADS * VD], where=ph)
    att_o = sb("att_o", [P, 4, T], where=ph)
    probs = sb("probs", [P, 2, T], where=ph)
    probsT = sb("probsT", [P, 2, NT, P], where=ph)
    stat = sb("stat", [P, 2, 4], where=ph)
    ph.close()
    ph = ExitStack()
    u_pad = sb("u_pad", [P, 4, CV_W - 1 + T], where=ph)
    cv_o = sb("cv_o", [P, 4, T], where=ph)
    m_hi = sb("m_hi", [P, KD, T], F32R, where=ph)
    m_lo = sb("m_lo", [P, KD, T], F32R, where=ph)
    ph.close()
    ph = ExitStack()
    act_f = sb("act_f", [P, 2, T], where=ph)
    act_hi = sb("act_hi", [P, F_TILES, T], F32R, where=ph)
    act_lo = sb("act_lo", [P, F_TILES, T], F32R, where=ph)
    gate_b = sb("gate_b", [P, 1, T], where=ph)
    logits = sb("logits", [P, NT, N_EXP], where=ph)
    gates = sb("gates", [P, NT, N_EXP], where=ph)
    g_sel = sb("g_sel", [P, NT, N_EXP], where=ph)
    top_v = sb("top_v", [P, NT, 8], where=ph)
    top_i = sb("top_i", [P, NT, 8], U32, where=ph)
    top_f = sb("top_f", [P, NT, 2], where=ph)
    top_w = sb("top_w", [P, NT, 2], where=ph)
    gate_w = sb("gate_w", [P, 1, NT, P], where=ph)
    ph.close()

    psum = ctx.enter_context(nc.psum_tensor("psum", [P, 8, 512], F32))

    def pair(t):
        return psum[:, 2 * (t % 2):2 * (t % 2) + 2, 0:HALF]

    def halves(ap):
        return ap.rearrange("p (h n) -> p h n", h=2)

    def work2(i):
        return psum[:, 4 + 2 * (i % 2):6 + 2 * (i % 2), 0:HALF]

    def bank4(b):
        return psum[:, b, :].rearrange("p (h n) -> p h n", h=4)

    def flat(b0, c0, n):
        return psum[:, b0:8, :].rearrange("p b n -> p (b n)")[:, c0:c0 + n]

    def v(name, i=0, rows=slice(0, P)):
        return vec[rows, VEC[name] + i:VEC[name] + i + 1]

    def bc(ap, axis, n):
        ap = ap.unsqueeze(axis)
        shape = list(ap.shape)
        shape[axis] = n
        return ap.broadcast_to(shape)

    def branch_src(n):
        return (qkv, att_o, cv_o)[n]

    raw_in = [sem(f"raw_in{j}") for j in range(RAW)]
    const_in = sem("const_in")
    vec_in = sem("vec_in")
    set_up = sem("set_up")
    hi_done = sem("hi_done")
    lo_done = sem("lo_done")
    tile_done = sem("tile_done")
    act_mix = sem("act_mix")
    dve_mix = sem("dve_mix")
    pe_mix = sem("pe_mix")
    act_ln = sem("act_ln")
    dve_ln = sem("dve_ln")
    pe_ln = sem("pe_ln")
    silu_done = sem("silu_done")
    act_done = sem("act_done")
    acth_done = sem("acth_done")
    actl_done = sem("actl_done")
    y_tmp = sem("y_tmp")
    y_done = sem("y_done")
    y_init = sem("y_init")
    rt_pe, rt_act, rt_dve = sem("rt_pe"), sem("rt_act"), sem("rt_dve")
    gb_copy, gb_pe, gb_ready = sem("gb_copy"), sem("gb_pe"), sem("gb_ready")
    out_done = sem("out_done")

    def gy(l, n, m):
        return l, "evac", TILE0[f"br{n}"] + 2 * m + 1

    EXP0 = [0, EXPERTS[0]]

    def panel0(l):
        return l * MIX_PANELS + EXP0[l] * PER_EXPERT

    def tile0(l):
        return l * MIX_TILES + EXP0[l] * PER_EXPERT

    block = ctx.enter_context(nc.Block())

    @block.sync
    def _(sp):
        sp.dma_start(acc[:], ins["h0"]).then_inc(const_in, 16)
        for name, dst in (("ident", ident), ("cum_mask", cum_mask), ("neg_ji", neg_ji), ("neg_qk", neg_qk),
                          ("level_mask", level_mask), ("meta_rows", meta_rows), ("rope", rope),
                          ("expert_no", expert_no), ("router", router)):
            sp.dma_start(dst[:], ins[name]).then_inc(const_in, 16)
        sp.dma_start(vec[:], ins["vec"][0]).then_inc(vec_in, 16)

        def load(slot, src, cols, count):
            sp.wait_ge(lo_done, count)
            sp.dma_start(raw[:, slot, 0:cols], src).then_inc(raw_in[slot], 16)

        for l in range(DEPTH):
            g0 = panel0(l)
            if l == 0:
                for j in range(RAW):
                    sp.dma_start(raw[:, j, 0:WIDE], ins["mix_panels"][0, j]).then_inc(raw_in[j], 16)
            with nc.sync.Fori(0, MIX_PANELS // RAW - (l == 0)) as i:
                for j in range(RAW):
                    q = i * RAW + j + (RAW if l == 0 else 0)
                    src = ins["mix_panels"][l, bass.ds(q, 1)].rearrange("a p n -> p (a n)")
                    load(j, src, WIDE, q + (g0 - RAW + 1))
            with nc.sync.Fori(0, EXPERTS[l] // 2) as i:
                for x in range(2):
                    for f in range(2 * F_TILES):
                        n = x * PER_EXPERT + f
                        src = ins["up_panels"][bass.ds(i * 2 + (EXP0[l] + x), 1), f].rearrange("a p n -> p (a n)")
                        load(n % RAW, src, WIDE, i * (2 * PER_EXPERT) + (g0 + MIX_PANELS + n - RAW + 1))
                    for m in range(KD):
                        n = x * PER_EXPERT + 2 * F_TILES + m
                        src = ins["down_panels"][bass.ds(i * 2 + (EXP0[l] + x), 1), m].rearrange("a p n -> p (a n)")
                        load(n % RAW, src, DEEP, i * (2 * PER_EXPERT) + (g0 + MIX_PANELS + n - RAW + 1))
            if l + 1 < DEPTH:
                sp.wait_ge(*at((l, "ln2", "out", KD - 1)))
                sp.dma_start(vec[:], ins["vec"][l + 1]).then_inc(vec_in, 16)
        for c in range(KD):
            sp.wait_ge(*at((DEPTH - 1, "ln2", "out", c)))
            sp.dma_start(out[:, c, :], acc[:, c, N_META:T]).then_inc(out_done, 16)
        sp.wait_ge(out_done, 16 * KD)

    @block.gpsimd
    def _(pool):
        nc.gpsimd.memset(ones[:], 1.0).then_inc(*mark("set_up", "ones"))
        nc.gpsimd.memset(eps[:], EPS).then_inc(*mark("set_up", "eps"))
        for l in range(DEPTH):
            if l:
                pool.wait_ge(lo_done, panel0(l))
            for p in range(MIX_PANELS):
                g = panel0(l) + p
                slot, s = g % RAW, g % 2
                pool.wait_ge(raw_in[slot], 16 * (g // RAW + 1))
                if p >= 2:
                    pool.wait_ge(*at((l, "tile", LAST_TILE[p - 2])))
                elif l > 0:
                    pool.wait_ge(tile_done, tile0(l) - 1 + p)
                nc.gpsimd.tensor_copy(w_hi[:, s, 0:WIDE], raw[:, slot, 0:WIDE]).then_inc(hi_done, 1)
                pool.wait_ge(hi_done, g + 1)
                nc.gpsimd.tensor_tensor(w_lo[:, s, 0:WIDE], raw[:, slot, 0:WIDE],
                                        w_hi[:, s, 0:WIDE].bitcast(F32), ALU.subtract).then_inc(lo_done, 1)

    @block.tensor
    def _(pe):
        pe.sem_inc(gb_pe, 1)
        last_read = {}

        def take(banks, *readers):
            waits = {}
            for b in banks:
                for label in last_read.get(b, ()):
                    s, n = at(label)
                    waits[id(s)] = (s, max(n, waits.get(id(s), (s, 0))[1]))
                last_read[b] = readers
            for s, n in waits.values():
                pe.wait_ge(s, n)

        def mm3(dst, w_h, w_l, x_h, x_l, start, stop):
            nc.tensor.matmul(dst, w_h, x_h, start=start, stop=False)
            nc.tensor.matmul(dst, w_l, x_h, start=False, stop=False)
            return nc.tensor.matmul(dst, w_h, x_l, start=False, stop=stop)

        def product(dst, s, b0, nb, x_h, x_l):
            for k in range(nb):
                cols = slice((b0 + k) * P, (b0 + k + 1) * P)
                for hf in range(2):
                    tok = slice(hf * HALF, (hf + 1) * HALF)
                    last = mm3(dst[:, hf, :], w_hi[:, s, cols], w_lo[:, s, cols], x_h[:, k, tok], x_l[:, k, tok],
                               k == 0, k == nb - 1)
            return last

        def sum_rows(dst, src, start, stop):
            for hf in range(2):
                last = nc.tensor.matmul(dst[:, hf, :], ones[:], src[:, hf * HALF:(hf + 1) * HALF],
                                        start=start, stop=stop)
            return last

        def tile_of(l, name, i, b0, nb, x_h, x_l, panel):
            t = TILE0[name] + i
            pe.wait_ge(lo_done, panel0(l) + panel + 1)
            bt = (tile0(l) + t) % 2
            take((2 * bt, 2 * bt + 1), (l, "evac", t))
            product(pair(bt), (panel0(l) + panel) % 2, b0, nb, x_h, x_l).then_inc(*mark("tile_done", (l, "tile", t)))

        def branch(l, n, p0):
            for i in range(4):
                for m in (2 * i, 2 * i + 1):
                    for part in range(2):
                        if part == 0:
                            tile_of(l, f"br{n}", 2 * m, 0, KD, h_hi, h_lo, p0 + 3 * i + m % 2)
                        else:
                            if i == 0 and m == 0:
                                pe.wait_ge(*at((l, "br", n)))
                            tile_of(l, f"br{n}", 2 * m + 1, 4 * (m % 2), 4, br_hi, br_lo, p0 + 3 * i + 2)

        for l in range(DEPTH):
            pe.wait_ge(*at((l, "h")))
            for i in range(12):
                tile_of(l, "qkv", i, 0, KD, h_hi, h_lo, i)
            t = TILE0["ba"]
            bt = (tile0(l) + t) % 2
            pe.wait_ge(lo_done, panel0(l) + 13)
            take((2 * bt, 2 * bt + 1), (l, "evac", t))
            s = (panel0(l) + 12) % 2
            for c in range(NT):
                for k in range(KD):
                    last = mm3(psum[:, 2 * bt, 8 * c:8 * c + 8], h_hi[:, k, WIN[c]:WIN[c] + P],
                               h_lo[:, k, WIN[c]:WIN[c] + P], w_hi[:, s, 8 * k:8 * k + 8],
                               w_lo[:, s, 8 * k:8 * k + 8], k == 0, k == KD - 1)
            last.then_inc(*mark("tile_done", (l, "tile", t)))
            for i in range(8):
                pe.wait_ge(*at((l, "qk_sq", i)))
                take((4 + 2 * (i % 2), 5 + 2 * (i % 2)), (l, "qk_rt", i))
                sum_rows(work2(i), tmp_s[:, i % 2, :], True, True).then_inc(*mark("pe_mix", (l, "qk_ss", i)))

            def chunk_setup(c, b):
                w = slice(WIN[c], WIN[c] + P)
                pe.wait_ge(*at((l, "gb", c)))
                take((4,), (l, "cum_s", c))
                nc.tensor.matmul(psum[:, 4, 0:4], cum_mask[:], g_tok[:, c, :], start=True, stop=True)
                nc.tensor.matmul(psum[:, 4, 4:8], ones[:], g_tok[:, c, :], start=True, stop=True)\
                    .then_inc(*mark("pe_mix", (l, "cum", c)))
                take((5,), (l, "diff", c), (l, "eB", c))
                for hd in range(4):
                    last = nc.tensor.matmul(bank4(5)[:, hd, :], wk[:, 0, hd, :], cum_mask[:], start=True, stop=True)
                last.then_inc(*mark("pe_mix", (l, "cumB", c)))
                take((6,), (l, "m1", c))
                for hd in range(4):
                    kk = qkv[:, 4 + hd, w]
                    last = nc.tensor.matmul(bank4(6)[:, hd, :], kk, kk, start=True, stop=True)
                last.then_inc(*mark("pe_mix", (l, "kk", c)))
                take((7,), (l, "qkg", c))
                for hd in range(4):
                    last = nc.tensor.matmul(bank4(7)[:, hd, :], qkv[:, 4 + hd, w], qkv[:, hd, w], start=True, stop=True)
                last.then_inc(*mark("pe_mix", (l, "qk", c)))
                take((0,), (l, "kdec", c))
                for hd in range(4):
                    last = nc.tensor.transpose(bank4(0)[:, hd, :], qkv[:, 4 + hd, w], ident[:])
                last.then_inc(*mark("pe_mix", (l, "ktok", c)))
                take((1,), (l, "vtok", c))
                for hd in range(4):
                    last = nc.tensor.transpose(bank4(1)[:, hd, :], qkv[:, 8 + hd, w], ident[:])
                last.then_inc(*mark("pe_mix", (l, "vtr", c)))
                pe.wait_ge(*at((l, "m1", c)))
                take((2,), (l, "aN", c))
                for hd in range(4):
                    last = nc.tensor.transpose(bank4(2)[:, hd, :], wk[:, 1, hd, :], ident[:])
                last.then_inc(*mark("pe_mix", (l, "aT", c)))

            def level(c, b, lv, n):
                x_b = n % 3
                pe.wait_ge(*at((l, "E", c, lv)))
                if lv:
                    pe.wait_ge(*at((l, "dN", c, lv - 1)))
                    pe.wait_ge(*at((l, "dT", c, lv - 1)))
                take((x_b,), (l, "X", c, lv))
                for hd in range(4):
                    last = nc.tensor.matmul(bank4(x_b)[:, hd, :], lvl_e[:, n % 3, hd, :],
                                            dT[:, b, hd, :] if lv else ident[:], start=True, stop=True)
                last.then_inc(*mark("pe_mix", (l, "Xp", c, lv)))

            def level_y(c, b, lv, n):
                y_b = 3 + n % 3
                pe.wait_ge(*at((l, "X", c, lv)))
                take((y_b,), (l, "dT", c, lv))
                for hd in range(4):
                    last = nc.tensor.matmul(bank4(y_b)[:, hd, :], dN[:, b, hd, :] if lv else ident[:],
                                            lvl_x[:, n % 3, hd, :], start=True, stop=True)
                last.then_inc(*mark("pe_mix", (l, "Yp", c, lv)))

            def level_t(c, b, lv, n):
                t_b = 6 + n % 2
                pe.wait_ge(*at((l, "dT", c, lv)))
                take((t_b,), (l, "dN", c, lv))
                for hd in range(4):
                    last = nc.tensor.transpose(bank4(t_b)[:, hd, :], dT[:, b, hd, :], ident[:])
                last.then_inc(*mark("pe_mix", (l, "Tp", c, lv)))

            def recur(c, b):
                s0, n = TILES[c]
                w = slice(WIN[c], WIN[c] + P)
                pe.wait_ge(*at((l, "ds", c - 1) if c else (l, "state0")))
                take((0,), (l, "r1", c))
                for hd in range(4):
                    last = nc.tensor.matmul(bank4(0)[:, hd, :], qkv[:, 4 + hd, w], state[:, hd, :],
                                            start=True, stop=True)
                last.then_inc(*mark("pe_mix", (l, "ks", c)))
                pe.wait_ge(*at((l, "R", c)))
                pe.wait_ge(*at((l, "TT", c)))
                take((1,), (l, "u", c))
                for hd in range(4):
                    last = nc.tensor.matmul(bank4(1)[:, hd, :], dT[:, b, hd, :], lvl_e[:, 0, hd, :],
                                            start=True, stop=True)
                last.then_inc(*mark("pe_mix", (l, "up", c)))
                pe.wait_ge(*at((l, "u", c)))
                take((3,), (l, "ds", c))
                for hd in range(4):
                    last = nc.tensor.matmul(bank4(3)[:, hd, :], kdec[:, b, hd, :], lvl_x[:, 0, hd, :],
                                            start=True, stop=True)
                last.then_inc(*mark("pe_mix", (l, "dsp", c)))
                take((2,), (l, "o", c))
                for hd in range(4):
                    nc.tensor.matmul(bank4(2)[:, hd, 0:n], state[:, hd, :], qkv[:, hd, s0:s0 + n],
                                     start=True, stop=False)
                    last = nc.tensor.matmul(bank4(2)[:, hd, 0:n], lvl_x[:, 0, hd, :], qkg[:, b, hd, 0:n],
                                            start=False, stop=True)
                last.then_inc(*mark("pe_mix", (l, "op", c)))

            for grp in ((0, 1, 2), (3, 4)):
                for b, c in enumerate(grp):
                    chunk_setup(c, b)
                n = 0
                for lv in range(LEVELS):
                    for b, c in enumerate(grp):
                        level(c, b, lv, n + b)
                    for b, c in enumerate(grp):
                        level_y(c, b, lv, n + b)
                    if lv < LEVELS - 1:
                        for b, c in enumerate(grp):
                            level_t(c, b, lv, n + b)
                    n += len(grp)
                for b, c in enumerate(grp):
                    recur(c, b)
            for hd in range(4):
                pe.wait_ge(*at((l, "o_sq", hd)))
                take((4 + 2 * (hd % 2), 5 + 2 * (hd % 2)), (l, "o_rt", hd))
                sum_rows(work2(hd), tmp_s[:, hd % 2, :], True, True).then_inc(*mark("pe_mix", (l, "o_ss", hd)))
            for i in range(4):
                tile_of(l, "z", i, 0, KD, h_hi, h_lo, 13 + i)
            branch(l, 0, 17)

            for i in range(4):
                tile_of(l, "c", i, 0, KD, h_hi, h_lo, 29 + i)
            pe.wait_ge(*at((l, "c_sq", 1)))
            take((4, 5), (l, "c_rt", 0))
            sum_rows(work2(0), tmp_s[:, 0, :], True, False)
            sum_rows(work2(0), tmp_s[:, 1, :], False, True).then_inc(*mark("pe_mix", (l, "c_ss", 0)))
            pe.wait_ge(*at((l, "c_sq", 2)))
            take((6, 7), (l, "c_rt", 1))
            sum_rows(work2(1), gate_s[:, 0, :], True, True).then_inc(*mark("pe_mix", (l, "c_ss", 1)))
            pe.wait_ge(*at((l, "cn", 1)))
            for i in range(HEADS):
                tile_of(l, "uq", i, 2 * (i % 4), 2, cn_hi, cn_lo, 33 + i // 4)
            pe.wait_ge(*at((l, "cn", 2)))
            for i in range(4):
                tile_of(l, "kn", i, i, 1, cn_hi[:, 2:3, :], cn_lo[:, 2:3, :], 35)
            s = (panel0(l) + 35) % 2
            for c in range(NT):
                t = TILE0["v"] + c
                bt = (tile0(l) + t) % 2
                take((2 * bt, 2 * bt + 1), (l, "evac", t))
                w = slice(WIN[c], WIN[c] + P)
                mm3(psum[:, 2 * bt, :], cn_hi[:, 2, w], cn_lo[:, 2, w], w_hi[:, s, 512:1024], w_lo[:, s, 512:1024],
                    True, True).then_inc(*mark("tile_done", (l, "tile", t)))
            items = [(hd, i) for hd in range(HEADS) for i in range(NT)]

            def scores(n):
                hd, i = items[n]
                q0, qn = TILES[i]
                nk = q0 + qn
                b = 4 + 2 * (n % 2)
                if i == 0:
                    pe.wait_ge(*at((l, "evac", TILE0["uq"] + hd)))
                    pe.wait_ge(*at((l, "q_sum", hd)))
                    pe.wait_ge(*at((l, "evac", TILE0["kn"] + hd // 2)))
                    pe.wait_ge(*at((l, "kr", hd) if hd else (l, "k_rope")))
                take((b, b + 1), (l, "exp", n))
                for k0, k1 in ((0, min(256, nk)), (256, nk)):
                    if k1 > k0:
                        last = nc.tensor.matmul(flat(b, 256 + k0, k1 - k0)[0:qn], qT[0:QK, hd, q0:q0 + qn],
                                                kT[0:QK, hd, k0:k1], start=True, stop=True)
                last.then_inc(*mark("pe_mix", (l, "s", n)))

            def turn(n):
                hd, i = items[n]
                qn = TILES[i][1]
                pe.wait_ge(*at((l, "p", n)))
                take((0, 1), (l, "pT", n))
                for j in range(i + 1):
                    k0, kn = TILES[j]
                    last = nc.tensor.transpose(flat(0, P * j, qn)[0:kn], probs[0:qn, n % 2, k0:k0 + kn],
                                               ident[0:qn, 0:qn])
                last.then_inc(*mark("pe_mix", (l, "t", n)))

            def values(n):
                hd, i = items[n]
                qn = TILES[i][1]
                pe.wait_ge(*at((l, "pT", n)))
                b = 2 + n % 2
                take((b,), (l, "oT", n))
                r = VD * (hd % 2)
                for j in range(i + 1):
                    kn = TILES[j][1]
                    last = nc.tensor.matmul(psum[r:r + VD, b, 0:qn], v_tok[0:kn, j, hd * VD:(hd + 1) * VD],
                                            probsT[0:kn, n % 2, j, 0:qn], start=(j == 0), stop=(j == i))
                last.then_inc(*mark("pe_mix", (l, "pv", n)))

            pe.wait_ge(*at((l, "evac", TILE0["v"] + NT - 1)))
            scores(0)
            for n in range(len(items)):
                if n + 1 < len(items):
                    scores(n + 1)
                turn(n)
                if n:
                    values(n - 1)
            values(len(items) - 1)
            branch(l, 1, 36)

            for i in range(8):
                tile_of(l, "cv", i, 0, KD, h_hi, h_lo, 48 + i)
            take((4, 5), (l, "cv_mu"))
            for i in range(4):
                pe.wait_ge(*at((l, "cv_o", i)))
                last = sum_rows(work2(0), cv_o[:, i, :], i == 0, i == 3)
            last.then_inc(*mark("pe_mix", (l, "cv_sum")))
            take((6, 7), (l, "cv_rt"))
            for i in range(4):
                pe.wait_ge(*at((l, "cv_sq", i)))
                last = sum_rows(work2(1), tmp_s[:, i % 2, :], i == 0, i == 3)
                last.then_inc(*mark("pe_mix", (l, "cv_ss", i)))
            branch(l, 2, 56)

            pe.wait_ge(*at((l, "m", KD - 1)))
            for i in range(KD):
                tile_of(l, "mix", i, 0, KD, m_hi, m_lo, 68 + i)

            def norm(which, wait):
                take((4, 5), (l, which, "mu"))
                for k in range(KD):
                    wait(k)
                    last = sum_rows(work2(0), acc[:, k, :], k == 0, k == KD - 1)
                last.then_inc(*mark("pe_ln", (l, which, "sum")))
                take((6, 7), (l, which, "rt"))
                for k in range(KD):
                    pe.wait_ge(*at((l, which, "sq", k)))
                    sum_rows(work2(1), tmp_s[:, k % 2, :], k == 0, k == KD - 1)\
                        .then_inc(*mark("pe_ln", (l, which, "ss", k)))

            norm("ln1", lambda k: pe.wait_ge(*at((l, "ln1", "x", k))))

            pe.wait_ge(*at((l, "h_mid")))
            if l == 1:
                take((4,), (l, "logits"))
                for c in range(NT):
                    for k in range(KD):
                        last = mm3(psum[:, 4, 8 * c:8 * c + 8], h_hi[:, k, WIN[c]:WIN[c] + P],
                                   h_lo[:, k, WIN[c]:WIN[c] + P], router_hi[:, k, :], router_lo[:, k, :],
                                   k == 0, k == KD - 1)
                last.then_inc(*mark("rt_pe", (l, "rt_pe")))
            e0 = EXP0[l]
            t0 = (l + 1) * MIX_TILES + EXP0[l] * PER_EXPERT
            g0 = (l + 1) * MIX_PANELS + EXP0[l] * PER_EXPERT
            take((0, 1, 2, 3, 6, 7))
            with nc.tensor.Fori(0, EXPERTS[l]) as e:
                if l == 1:
                    pe.wait_ge(gb_copy, e * NT + NT)
                    pe.wait_ge(gb_ready, e + 1)
                    for c in range(NT):
                        s0, n = TILES[c]
                        dst = psum[:, 6, s0:s0 + n] if s0 + n <= HALF else (psum[:, 7, s0 - HALF:s0 - HALF + n]
                                                                           if s0 >= HALF else None)
                        if dst is None:
                            n1 = HALF - s0
                            nc.tensor.matmul(psum[:, 6, s0:HALF], gate_w[:, 0, c, :], ident[:, 0:n1],
                                             start=True, stop=True)
                            last = nc.tensor.matmul(psum[:, 7, 0:n - n1], gate_w[:, 0, c, :], ident[:, n1:n],
                                                    start=True, stop=True)
                        else:
                            last = nc.tensor.matmul(dst, gate_w[:, 0, c, :], ident[:, 0:n], start=True, stop=True)
                    last.then_inc(gb_pe, 1)
                with nc.tensor.Fori(0, F_TILES) as f:
                    for part in range(2):
                        pe.wait_ge(lo_done, e * PER_EXPERT + f * 2 + (g0 + part + 1))
                        if part == 0:
                            pe.wait_ge(silu_done, (e + e0) * F_TILES + f + 1)
                            pe.wait_ge(y_done, (e + e0) * KD + 1)
                        else:
                            pe.wait_ge(act_done, (e + e0) * F_TILES + f + 1)
                        product(pair(part), part, 0, KD, h_hi, h_lo).then_inc(tile_done, 1)
                with nc.tensor.Fori(0, KD // 2) as m2:
                    for part in range(2):
                        pe.wait_ge(actl_done, (e + e0) * F_TILES + F_TILES)
                        pe.wait_ge(lo_done, e * PER_EXPERT + m2 * 2 + (g0 + 2 * F_TILES + part + 1))
                        pe.wait_ge(y_done, (e + e0) * KD + m2 * 2 + 1)
                        product(pair(part), part, 0, F_TILES, act_hi, act_lo).then_inc(tile_done, 1)
            counts.raised["tile_done"] += EXPERTS[l] * PER_EXPERT
            norm("ln2", lambda k: pe.wait_ge(y_done, 1 + (e0 + EXPERTS[l]) * KD - (KD - 1 - k)))

    @block.scalar
    def _(act):
        def fn(out_, in_, func, sem_, label, **kw):
            return nc.scalar.activation(out_, in_, func, **kw).then_inc(*mark(sem_, label))

        act.sem_inc(silu_done, 1)
        act.wait_ge(*at("eps"))
        for l in range(DEPTH):
            if l == 0:
                act.wait_ge(const_in, 160)
                for k in range(KD):
                    fn(h_hi[:, k, :], acc[:, k, :], ACT.Copy, "act_ln", ("h0_hi", k))
            act.wait_ge(vec_in, 16 * (l + 1))
            for i in range(12 + 2):
                if i < 12:
                    t = TILE0["qkv"] + i
                    act.wait_ge(*at((l, "tile", t)))
                    if i >= 2:
                        act.wait_ge(*at((l, "conv", i - 2)))
                    fn(halves(x_pad[:, i % 2, 3:3 + T]), pair(tile0(l) + t), ACT.Copy, "act_mix", (l, "evac", t))
                if i >= 1 and i - 1 < 12:
                    j = i - 1
                    act.wait_ge(*at((l, "conv", j)))
                    fn(qkv[:, j, :], conv_o[:, j % 2, :], ACT.Silu, "act_mix", (l, "qkv", j))
            t = TILE0["ba"]
            act.wait_ge(*at((l, "tile", t)))
            fn(ba[:].rearrange("p a b -> p (a b)"), psum[:, 2 * ((tile0(l) + t) % 2), 0:8 * NT], ACT.Copy,
               "act_mix", (l, "evac", t))
            act.wait_ge(*at((l, "qkv", 11)))
            for i in range(8 + 1):
                if i < 8:
                    if i >= 2:
                        act.wait_ge(*at((l, "qk_ss", i - 2)))
                    fn(tmp_s[:, i % 2, :], qkv[:, i, :], ACT.Square, "act_mix", (l, "qk_sq", i))
                if i >= 1:
                    j = i - 1
                    act.wait_ge(*at((l, "qk_ss", j)))
                    if j >= 2:
                        act.wait_ge(*at((l, "qkn", j - 2)))
                    fn(halves(gate_s[:, j % 2, :]), work2(j), ACT.Sqrt, "act_mix", (l, "qk_rt", j), bias=eps[:, 0:1])
            fn(b_tok[:], ba[:, :, 0:4], ACT.Sigmoid, "act_mix", (l, "beta"))
            act.wait_ge(*at((l, "a_dt")))
            fn(sp2[:], sp1[:], ACT.Abs, "act_mix", (l, "a_abs"))
            act.wait_ge(*at((l, "a_abs")))
            fn(sp2[:], sp2[:], ACT.Exp, "act_mix", (l, "a_exp"), scale=-1.0)
            fn(ea[:], vec[:, VEC["a_log"]:VEC["a_log"] + 4], ACT.Exp, "act_mix", (l, "ea"))
            act.wait_ge(*at((l, "a_exp")))
            fn(sp2[:], sp2[:], ACT.Ln, "act_mix", (l, "a_ln"), bias=1.0)

            def chunk_setup(c, b):
                act.wait_ge(*at((l, "cum", c)))
                fn(cums[:, c, :], psum[:, 4, 0:8], ACT.Copy, "act_mix", (l, "cum_s", c))
                act.wait_ge(*at((l, "cum_s", c)))
                fn(ecum[:, c, :], cums[:, c, :], ACT.Exp, "act_mix", (l, "ecum", c))
                act.wait_ge(*at((l, "tot", c)))
                fn(eneg[:, c, :], eneg[:, c, :], ACT.Exp, "act_mix", (l, "eneg", c))
                act.wait_ge(*at((l, "diff", c)))
                fn(lvl_x[:, 0], bank4(5), ACT.Exp, "act_mix", (l, "eB", c))
                act.wait_ge(*at((l, "diffm", c)))
                fn(wk[:, 1], wk[:, 1], ACT.Exp, "act_mix", (l, "gam", c))
                act.wait_ge(*at((l, "vtr", c)))
                fn(vtok[:, b], bank4(1), ACT.Copy, "act_mix", (l, "vtok", c))

            def level(c, b, lv, n):
                act.wait_ge(*at((l, "Xp", c, lv)))
                fn(lvl_x[:, n % 3], bank4(n % 3), ACT.Copy, "act_mix", (l, "X", c, lv))

            def level_t(c, b, lv, n):
                act.wait_ge(*at((l, "Tp", c, lv)))
                fn(dN[:, b], bank4(6 + n % 2), ACT.Copy, "act_mix", (l, "dN", c, lv))

            def recur(c, b):
                s0, n = TILES[c]
                act.wait_ge(*at((l, "up", c)))
                fn(lvl_x[:, 0], bank4(1), ACT.Copy, "act_mix", (l, "u", c))
                act.wait_ge(*at((l, "op", c)))
                fn(qkv[:, 0:4, s0:s0 + n], bank4(2)[:, :, 0:n], ACT.Copy, "act_mix", (l, "o", c))

            for grp in ((0, 1, 2), (3, 4)):
                for b, c in enumerate(grp):
                    chunk_setup(c, b)
                n = 0
                for lv in range(LEVELS):
                    for b, c in enumerate(grp):
                        level(c, b, lv, n + b)
                    if lv < LEVELS - 1:
                        for b, c in enumerate(grp):
                            level_t(c, b, lv, n + b)
                    n += len(grp)
                for b, c in enumerate(grp):
                    recur(c, b)
            act.wait_ge(*at((l, "o", NT - 1)))
            for i in range(4 + 1):
                if i < 4:
                    if i >= 2:
                        act.wait_ge(*at((l, "o_ss", i - 2)))
                    fn(tmp_s[:, i % 2, :], qkv[:, i, :], ACT.Square, "act_mix", (l, "o_sq", i))
                if i >= 1:
                    j = i - 1
                    act.wait_ge(*at((l, "o_ss", j)))
                    fn(halves(qkv[:, 4 + j, :]), work2(j), ACT.Sqrt, "act_mix", (l, "o_rt", j),
                       bias=eps[:, 0:1], scale=1.0 / P)
            for i in range(4):
                t = TILE0["z"] + i
                act.wait_ge(*at((l, "tile", t)))
                fn(halves(qkv[:, 8 + i, :]), pair(tile0(l) + t), ACT.Silu, "act_mix", (l, "evac", t))

            def split_hi(n):
                for i in range(4):
                    act.wait_ge(*at((l, "br_f", n, i) if n != 1 else (l, "oT", HEADS * NT - 1)))
                    fn(br_hi[:, i, :], branch_src(n)[:, i, :], ACT.Copy, "act_mix", (l, "br_hi", n, i))

            def branch(n):
                for m in range(KD):
                    t = TILE0[f"br{n}"] + 2 * m
                    act.wait_ge(*at((l, "tile", t)))
                    if m >= 2:
                        act.wait_ge(*at(gy(l, n, m - 2)))
                    fn(halves(gate_s[:, m % 2, :]), pair(tile0(l) + t), ACT.Sigmoid, "act_mix", (l, "evac", t))

            split_hi(0)
            branch(0)

            for i in range(3):
                t = TILE0["c"] + i
                act.wait_ge(*at((l, "tile", t)))
                fn(halves(c_f[:, i, :]), pair(tile0(l) + t), ACT.Copy, "act_mix", (l, "evac", t))
                act.wait_ge(*at((l, "evac", t)))
                if i == 2:
                    act.wait_ge(*at(gy(l, 0, KD - 1)))
                fn(tmp_s[:, i, :] if i < 2 else gate_s[:, 0, :], c_f[:, i, :], ACT.Square, "act_mix", (l, "c_sq", i))
            act.wait_ge(*at((l, "c_ss", 0)))
            fn(halves(qT[:, 0, :]), work2(0), ACT.Sqrt, "act_mix", (l, "c_rt", 0), bias=eps[:, 0:1], scale=1 / 256)
            act.wait_ge(*at((l, "c_ss", 1)))
            fn(halves(qT[:, 1, :]), work2(1), ACT.Sqrt, "act_mix", (l, "c_rt", 1), bias=eps[:, 0:1], scale=1 / 128)
            for i in range(3):
                act.wait_ge(*at((l, "cf", i)))
                fn(cn_hi[:, i, :], c_f[:, i, :], ACT.Copy, "act_mix", (l, "cn_hi", i))
            act.wait_ge(*at((l, "k_rope")))
            for hd in range(1, HEADS):
                fn(kT[NOPE:QK, hd, :], kT[NOPE:QK, 0, :], ACT.Copy, "act_mix", (l, "kr", hd))
            for hd in range(HEADS):
                t = TILE0["uq"] + hd
                act.wait_ge(*at((l, "tile", t)))
                act.wait_ge(*at((l, "q_rope", hd)))
                if hd < 2:
                    act.wait_ge(*at((l, "cf", 2)))
                fn(halves(qT[0:NOPE, hd, :]), pair(tile0(l) + t)[0:NOPE], ACT.Copy, "act_mix", (l, "evac", t))
            for i in range(4):
                t = TILE0["kn"] + i
                act.wait_ge(*at((l, "tile", t)))
                fn(halves(kT[0:NOPE, 2 * i, :]), pair(tile0(l) + t)[0:NOPE], ACT.Copy, "act_mix", (l, "kn0", i))
                fn(halves(kT[0:NOPE, 2 * i + 1, :]), pair(tile0(l) + t)[NOPE:P], ACT.Copy, "act_mix", (l, "evac", t))
            for c in range(NT):
                t = TILE0["v"] + c
                act.wait_ge(*at((l, "tile", t)))
                fn(v_tok[:, c, :], psum[:, 2 * ((tile0(l) + t) % 2), :], ACT.Copy, "act_mix", (l, "evac", t))
            items = [(hd, i) for hd in range(HEADS) for i in range(NT)]

            def pt_evac(n):
                hd, i = items[n]
                qn = TILES[i][1]
                act.wait_ge(*at((l, "t", n)))
                if n >= 2:
                    act.wait_ge(*at((l, "pv", n - 2)))
                fn(probsT[0:N_META, n % 2, 0, 0:qn], flat(0, 0, qn)[0:N_META], ACT.Copy, "act_mix",
                   (l, "pT0", n) if i else (l, "pT", n))
                if i:
                    fn(probsT[:, n % 2, 1:i + 1, :], flat(0, P, P * i).rearrange("p (j n) -> p j n", n=P), ACT.Copy,
                       "act_mix", (l, "pT", n))

            def o_evac(n):
                hd, i = items[n]
                q0, qn = TILES[i]
                r = VD * (hd % 2)
                act.wait_ge(*at((l, "pv", n)))
                fn(att_o[r:r + VD, hd // 2, q0:q0 + qn], psum[r:r + VD, 2 + n % 2, 0:qn], ACT.Copy, "act_mix",
                   (l, "oT", n))

            for n in range(len(items) + 2):
                if n < len(items):
                    hd, i = items[n]
                    q0, qn = TILES[i]
                    nk = q0 + qn
                    act.wait_ge(*at((l, "nmax", n)))
                    if n >= 2:
                        act.wait_ge(*at((l, "t", n - 2)))
                    fn(probs[0:qn, n % 2, 0:nk], flat(4 + 2 * (n % 2), 256, nk)[0:qn], ACT.Exp, "act_mix",
                       (l, "exp", n), bias=stat[0:qn, n % 2, 1:2], scale=QK ** -0.5,
                       accum_out=stat[0:qn, n % 2, 2:3])
                if 1 <= n <= len(items):
                    pt_evac(n - 1)
                if n >= 2:
                    o_evac(n - 2)
            split_hi(1)
            branch(1)

            for i in range(4):
                t = TILE0["cv"] + 2 * i + 1
                act.wait_ge(*at((l, "tile", t)))
                if i < 2:
                    act.wait_ge(*at(gy(l, 1, KD - 1)))
                else:
                    act.wait_ge(*at((l, "evac", TILE0["cv"] + 2 * i - 4)))
                fn(halves(gate_s[:, i % 2, :]), pair(tile0(l) + t), ACT.Sigmoid, "act_mix", (l, "evac", t))
            act.wait_ge(*at((l, "cv_sum")))
            fn(halves(gate_s[:, 0, :]), work2(0), ACT.Copy, "act_mix", (l, "cv_mu"), scale=1 / 512)
            for i in range(4):
                act.wait_ge(*at((l, "cv_c", i)))
                if i >= 2:
                    act.wait_ge(*at((l, "cv_ss", i - 2)))
                fn(tmp_s[:, i % 2, :], cv_o[:, i, :], ACT.Square, "act_mix", (l, "cv_sq", i))
            act.wait_ge(*at((l, "cv_ss", 3)))
            fn(halves(gate_s[:, 1, :]), work2(1), ACT.Sqrt, "act_mix", (l, "cv_rt"), bias=eps[:, 0:1], scale=1 / 512)
            for i in range(4):
                act.wait_ge(*at((l, "cv_n", i)))
                fn(cv_o[:, i, :], cv_o[:, i, :], ACT.Silu, "act_mix", (l, "br_f", 2, i), bias=v("cvlb", i))
            split_hi(2)
            branch(2)
            for m in range(KD):
                act.wait_ge(*at((l, "merged", m)))
                fn(m_hi[:, m, :], acc[:, m, :], ACT.Copy, "act_mix", (l, "m_hi", m))

            def norm(which):
                act.wait_ge(*at((l, which, "sum")))
                fn(halves(gate_s[:, 0, :]), work2(0), ACT.Copy, "act_ln", (l, which, "mu"), scale=1 / D)
                for k in range(KD):
                    act.wait_ge(*at((l, which, "c", k)))
                    if k >= 2:
                        act.wait_ge(*at((l, which, "ss", k - 2)))
                    fn(tmp_s[:, k % 2, :], acc[:, k, :], ACT.Square, "act_ln", (l, which, "sq", k))
                act.wait_ge(*at((l, which, "ss", KD - 1)))
                fn(halves(gate_s[:, 1, :]), work2(1), ACT.Sqrt, "act_ln", (l, which, "rt"), bias=eps[:, 0:1],
                   scale=1 / D)
                for k in range(KD):
                    act.wait_ge(*at((l, which, "n", k)))
                    fn(acc[:, k, :], acc[:, k, :], ACT.Identity, "act_ln", (l, which, "out", k),
                       bias=v(which + "b", k))
                    if not (which == "ln2" and l == DEPTH - 1):
                        act.wait_ge(*at((l, which, "out", k)))
                        fn(h_hi[:, k, :], acc[:, k, :], ACT.Copy, "act_ln", (l, which, "hi", k))

            norm("ln1")

            e0 = EXP0[l]
            t0 = (l + 1) * MIX_TILES + EXP0[l] * PER_EXPERT
            g0 = (l + 1) * MIX_PANELS + EXP0[l] * PER_EXPERT
            if l == 1:
                act.wait_ge(*at((l, "rt_pe")))
                fn(logits[:].rearrange("p a b -> p (a b)"), psum[:, 4, 0:8 * NT], ACT.Copy, "rt_act", (l, "logits"))
                act.wait_ge(*at((l, "w_arg")))
                fn(top_w[:, :, 1:2], top_w[:, :, 1:2], ACT.Exp, "rt_act", (l, "w_exp"))
            act.wait_ge(lo_done, g0)

            def heads(slot_panel, s, cols, raw_slot, raw_count, used):
                act.wait_ge(raw_in[raw_slot], raw_count)
                act.wait_ge(tile_done, used)
                nc.scalar.activation(w_hi[:, s, 0:cols], raw[:, raw_slot, 0:cols], ACT.Copy).then_inc(hi_done, 1)

            def panel_heads(i2, n):
                cols = WIDE if n % PER_EXPERT < 2 * F_TILES else DEEP
                heads(None, n % 2, cols, n % RAW, i2 * (60 // RAW * 16) + 16 * ((g0 + n) // RAW + 1),
                      i2 * 60 + (t0 + n - 1))

            with nc.scalar.Fori(0, EXPERTS[l] // 2) as i2:
                panel_heads(i2, 0)
                panel_heads(i2, 1)
                for x in range(2):
                    for f in range(F_TILES):
                        n = x * PER_EXPERT + 2 * f
                        cnt = i2 * (2 * F_TILES) + ((e0 + x) * F_TILES + f)
                        panel_heads(i2, n + 2)
                        act.wait_ge(tile_done, i2 * 60 + (t0 + n + 1))
                        if (e0 + x) * F_TILES + f >= 2:
                            act.wait_ge(act_done, cnt)
                        nc.scalar.activation(halves(gate_s[:, f % 2, :]), pair(0), ACT.Silu).then_inc(silu_done, 1)
                        panel_heads(i2, n + 3)
                        act.wait_ge(act_done, cnt + 2)
                        nc.scalar.activation(act_hi[:, f, :], act_f[:, f % 2, :], ACT.Copy).then_inc(acth_done, 1)
                    for m in range(KD):
                        n = x * PER_EXPERT + 2 * F_TILES + m
                        if n + 2 < 60:
                            panel_heads(i2, n + 2)
            norm("ln2")

    @block.vector
    def _(dve):
        def tt(out_, a, b, op, sem_, label):
            return nc.vector.tensor_tensor(out_, a, b, op).then_inc(*mark(sem_, label))

        def ts(out_, a, s1, s2, op0, op1, sem_, label):
            if s2 is None:
                return nc.vector.tensor_scalar(out_, a, s1, None, op0).then_inc(*mark(sem_, label))
            return nc.vector.tensor_scalar(out_, a, s1, s2, op0, op1).then_inc(*mark(sem_, label))

        def stt(out_, a, s, b, op0, op1, sem_, label):
            return nc.vector.scalar_tensor_tensor(out=out_, in0=a, scalar=s, in1=b, op0=op0, op1=op1)\
                .then_inc(*mark(sem_, label))

        def remainder(lo, full, hi, sem_, label):
            return tt(lo, full, hi.bitcast(F32), ALU.subtract, sem_, label)

        for s_ in (act_done, y_done, gb_ready):
            dve.sem_inc(s_, 1)
        dve.wait_ge(const_in, 160)
        nc.vector.tensor_copy(router_hi[:], router[:]).then_inc(*mark("rt_dve", "router_hi"))
        dve.wait_ge(*at("router_hi"))
        remainder(router_lo[:], router[:], router_hi[:], "rt_dve", "router_lo")
        for l in range(DEPTH):
            dve.wait_ge(vec_in, 16 * (l + 1))
            if l == 0:
                for k in range(KD):
                    dve.wait_ge(*at(("h0_hi", k)))
                    remainder(h_lo[:, k, :], acc[:, k, :], h_hi[:, k, :], "dve_ln",
                              ("h0_lo", k) if k < KD - 1 else (0, "h"))
            nc.vector.memset(x_pad[:, :, 0:3], 0.0).then_inc(*mark("dve_mix", (l, "pad")))
            dve.wait_ge(*at((l, "pad")))
            for i in range(12):
                t = TILE0["qkv"] + i
                dve.wait_ge(*at((l, "evac", t)))
                if i >= 2:
                    dve.wait_ge(*at((l, "qkv", i - 2)))
                for w in range(4):
                    src = x_pad[:, i % 2, w:w + T]
                    label = (l, "conv", i) if w == 3 else (l, "conv", i, w)
                    if w == 0:
                        ts(conv_o[:, i % 2, :], src, v("conv", 4 * i), None, ALU.mult, None, "dve_mix", label)
                    else:
                        dve.wait_ge(*at((l, "conv", i, w - 1)))
                        stt(conv_o[:, i % 2, :], src, v("conv", 4 * i + w), conv_o[:, i % 2, :], ALU.mult, ALU.add,
                            "dve_mix", label)
            for i in range(8):
                dve.wait_ge(*at((l, "qk_rt", i)))
                nc.vector.reciprocal(gate_s[:, i % 2, :], gate_s[:, i % 2, :]).then_inc(*mark("dve_mix", (l, "qk_r", i)))
                dve.wait_ge(*at((l, "qk_r", i)))
                dve.wait_ge(*at((l, "qkv", i)))
                stt(qkv[:, i, :], qkv[:, i, :], P ** -0.5 if i < 4 else 1.0, gate_s[:, i % 2, :], ALU.mult, ALU.mult,
                    "dve_mix", (l, "qkn", i))
            dve.wait_ge(*at((l, "evac", TILE0["ba"])))
            tt(sp1[:], ba[:, :, 4:8], bc(vec[:, VEC["dt"]:VEC["dt"] + 4], 1, NT), ALU.add, "dve_mix", (l, "a_dt"))
            dve.wait_ge(*at((l, "a_ln")))
            stt(sp1[:], sp1[:], 0.0, sp2[:], ALU.max, ALU.add, "dve_mix", (l, "sp"))
            dve.wait_ge(*at((l, "sp")))
            stt(sp1[:], sp1[:], -1.0, bc(ea[:], 1, NT), ALU.mult, ALU.mult, "dve_mix", (l, "g_all"))
            dve.wait_ge(*at((l, "g_all")))
            tt(g_tok[:], sp1[:], meta_rows[:], ALU.mult, "dve_mix", (l, "g"))
            tt(b_tok[:], b_tok[:], meta_rows[:], ALU.mult, "dve_mix", (l, "beta_m"))
            dve.wait_ge(*at((l, "qkn", 7)))
            nc.vector.memset(state[:], 0.0).then_inc(*mark("dve_mix", (l, "state0")))
            dve.wait_ge(*at((l, "state0")))

            def chunk_setup(c, b):
                s0, n = TILES[c]
                if c:
                    dve.wait_ge(*at((l, "cumB", c - 1)))
                nc.vector.tensor_copy(wk[:, 0], bc(g_tok[:, c, :], 2, P)).then_inc(*mark("dve_mix", (l, "gb", c)))
                dve.wait_ge(*at((l, "cum_s", c)))
                tt(eneg[:, c, :], cums[:, c, 4:8], cums[:, c, 0:4], ALU.subtract, "dve_mix", (l, "tot", c))
                dve.wait_ge(*at((l, "cumB", c)))
                if c:
                    dve.wait_ge(*at((l, "aT", c - 1)))
                tt(wk[:, 1], bank4(5), bc(cums[:, c, 0:4], 2, P), ALU.subtract, "dve_mix", (l, "diff", c))
                dve.wait_ge(*at((l, "diff", c)))
                tt(wk[:, 1], wk[:, 1], bc(neg_ji[:], 1, 4), ALU.add, "dve_mix", (l, "diffm", c))
                dve.wait_ge(*at((l, "gam", c)))
                dve.wait_ge(*at((l, "qk", c)))
                tt(qkg[:, b], bank4(7), wk[:, 1], ALU.mult, "dve_mix", (l, "qkg", c))
                dve.wait_ge(*at((l, "qkg", c)))
                dve.wait_ge(*at((l, "kk", c)))
                tt(wk[:, 1], bank4(6), wk[:, 1], ALU.mult, "dve_mix", (l, "m1", c))
                dve.wait_ge(*at((l, "eB", c)))
                tt(qkv[:, 0:4, s0:s0 + n], qkv[:, 0:4, s0:s0 + n], lvl_x[:, 0, :, 0:n], ALU.mult, "dve_mix",
                   (l, "qdec", c))
                dve.wait_ge(*at((l, "eneg", c)))
                dve.wait_ge(*at((l, "ktok", c)))
                tt(kdec[:, b], bank4(0), bc(eneg[:, c, :], 2, P), ALU.mult, "dve_mix", (l, "kdec", c))
                dve.wait_ge(*at((l, "aT", c)))
                tt(aN[:, b], bank4(2), bc(b_tok[:, c, :], 2, P), ALU.mult, "dve_mix", (l, "aN", c))
                dve.wait_ge(*at((l, "aN", c)))
                dve.wait_ge(*at((l, "qdec", c)))

            def level_e(c, b, lv, n):
                tt(lvl_e[:, n % 3], aN[:, b], bc(level_mask[:, lv, :], 1, 4), ALU.mult, "dve_mix", (l, "E", c, lv))

            def level(c, b, lv, n):
                dve.wait_ge(*at((l, "Yp", c, lv)))
                base = dT[:, b] if lv else bc(ident[:], 1, 4)
                if lv:
                    dve.wait_ge(*at((l, "dT", c, lv - 1)))
                tt(dT[:, b], base, bank4(3 + n % 3), ALU.subtract, "dve_mix", (l, "dT", c, lv))

            def recur(c, b):
                dve.wait_ge(*at((l, "dT", c, LEVELS - 1)))
                tt(dT[:, b], dT[:, b], bc(b_tok[:, c, :], 2, P), ALU.mult, "dve_mix", (l, "TT", c))
                dve.wait_ge(*at((l, "ks", c)))
                dve.wait_ge(*at((l, "ecum", c)))
                tt(lvl_e[:, 0], bank4(0), bc(ecum[:, c, 0:4], 2, P), ALU.mult, "dve_mix", (l, "r1", c))
                dve.wait_ge(*at((l, "r1", c)))
                dve.wait_ge(*at((l, "vtok", c)))
                tt(lvl_e[:, 0], vtok[:, b], lvl_e[:, 0], ALU.subtract, "dve_mix", (l, "R", c))
                dve.wait_ge(*at((l, "op", c)))
                if c:
                    dve.wait_ge(*at((l, "ds", c - 1)))
                tt(state[:], state[:], bc(ecum[:, c, 4:8], 2, P), ALU.mult, "dve_mix", (l, "sd", c))
                dve.wait_ge(*at((l, "dsp", c)))
                dve.wait_ge(*at((l, "sd", c)))
                tt(state[:], state[:], bank4(3), ALU.add, "dve_mix", (l, "ds", c))

            for grp in ((0, 1, 2), (3, 4)):
                for b, c in enumerate(grp):
                    chunk_setup(c, b)
                seq = [(lv, b, c, lv * len(grp) + b) for lv in range(LEVELS) for b, c in enumerate(grp)]
                ahead = len(grp)
                for x in range(len(seq) + ahead):
                    if x < len(seq):
                        lv, b, c, n = seq[x]
                        if x >= 3:
                            dve.wait_ge(*at((l, "Xp", seq[x - 3][2], seq[x - 3][0])))
                        level_e(c, b, lv, n)
                    if x >= ahead:
                        lv, b, c, n = seq[x - ahead]
                        level(c, b, lv, n)
                for b, c in enumerate(grp):
                    recur(c, b)
            for i in range(4):
                dve.wait_ge(*at((l, "o_rt", i)))
                nc.vector.reciprocal(qkv[:, 4 + i, :], qkv[:, 4 + i, :]).then_inc(*mark("dve_mix", (l, "o_r", i)))
                dve.wait_ge(*at((l, "o_r", i)))
                stt(qkv[:, i, :], qkv[:, i, :], v("o_norm"), qkv[:, 4 + i, :], ALU.mult, ALU.mult, "dve_mix",
                    (l, "o_n", i))
            for i in range(4):
                dve.wait_ge(*at((l, "evac", TILE0["z"] + i)))
                dve.wait_ge(*at((l, "o_n", i)))
                tt(qkv[:, i, :], qkv[:, i, :], qkv[:, 8 + i, :], ALU.mult, "dve_mix", (l, "br_f", 0, i))

            def split_lo(n):
                for i in range(4):
                    dve.wait_ge(*at((l, "br_hi", n, i)))
                    remainder(br_lo[:, i, :], branch_src(n)[:, i, :], br_hi[:, i, :], "dve_mix",
                              (l, "br", n) if i == 3 else (l, "br_lo", n, i))

            def branch(n):
                for m in range(KD):
                    t = TILE0[f"br{n}"] + 2 * m + 1
                    dve.wait_ge(*at((l, "evac", t - 1)))
                    dve.wait_ge(*at((l, "tile", t)))
                    if n == 0:
                        tt(halves(acc[:, m, :]), pair(tile0(l) + t), halves(gate_s[:, m % 2, :]), ALU.mult, "dve_mix",
                           (l, "evac", t))
                    else:
                        if m >= 2:
                            dve.wait_ge(*at((l, "merge", n, m - 2) if n == 1 else (l, "merged", m - 2)))
                        tt(halves(tmp_s[:, m % 2, :]), pair(tile0(l) + t), halves(gate_s[:, m % 2, :]), ALU.mult,
                           "dve_mix", (l, "evac", t))
                        dve.wait_ge(*at((l, "evac", t)))
                        tt(acc[:, m, :], acc[:, m, :], tmp_s[:, m % 2, :], ALU.add, "dve_mix",
                           (l, "merge", n, m) if n == 1 else (l, "merged", m))

            split_lo(0)
            branch(0)

            t = TILE0["c"] + 3
            dve.wait_ge(*at((l, "tile", t)))
            dve.wait_ge(*at(gy(l, 0, KD - 1)))
            kr = pair(tile0(l) + t)
            r0, r1 = slice(NOPE, QK), slice(QK, P)
            tt(halves(kT[r0, 0, :]), kr[r0], halves(rope[r0, :]), ALU.mult, "dve_mix", (l, "kr_c"))
            tt(halves(kT[r0, 1, :]), kr[r1], halves(rope[r1, :]), ALU.mult, "dve_mix", (l, "evac", t))
            dve.wait_ge(*at((l, "kr_c")))
            dve.wait_ge(*at((l, "evac", t)))
            tt(kT[r0, 0, :], kT[r0, 0, :], kT[r0, 1, :], ALU.add, "dve_mix", (l, "k_rope"))
            for i in range(3):
                r = qT[:, i // 2, :]
                if i != 1:
                    dve.wait_ge(*at((l, "c_rt", i // 2)))
                    nc.vector.reciprocal(r, r).then_inc(*mark("dve_mix", (l, "c_r", i // 2)))
                    dve.wait_ge(*at((l, "c_r", i // 2)))
                stt(c_f[:, i, :], c_f[:, i, :], v("q_norm", i) if i < 2 else v("kv_norm"), r, ALU.mult, ALU.mult,
                    "dve_mix", (l, "cf", i))
            for i in range(3):
                dve.wait_ge(*at((l, "cn_hi", i)))
                remainder(cn_lo[:, i, :], c_f[:, i, :], cn_hi[:, i, :], "dve_mix", (l, "cn", i))
            for hd in range(HEADS):
                t = TILE0["uq"] + hd
                dve.wait_ge(*at((l, "tile", t)))
                if hd < 2:
                    dve.wait_ge(*at((l, "cf", 2)))
                if hd >= 1:
                    dve.wait_ge(*at((l, "q_sum", hd - 1)))
                qr = pair(tile0(l) + t)
                tt(halves(qT[r0, hd, :]), qr[r0], halves(rope[r0, :]), ALU.mult, "dve_mix", (l, "q_c", hd))
                tt(halves(c_f[r0, 0, :]), qr[r1], halves(rope[r1, :]), ALU.mult, "dve_mix", (l, "q_rope", hd))
                dve.wait_ge(*at((l, "q_rope", hd)))
                tt(qT[r0, hd, :], qT[r0, hd, :], c_f[r0, 0, :], ALU.add, "dve_mix", (l, "q_sum", hd))
            items = [(hd, i) for hd in range(HEADS) for i in range(NT)]
            SC = QK ** -0.5

            def normalise(n):
                hd, i = items[n]
                q0, qn = TILES[i]
                nk = q0 + qn
                dve.wait_ge(*at((l, "exp", n)))
                st = stat[0:qn, n % 2]
                nc.vector.reciprocal(st[:, 3:4], st[:, 2:3]).then_inc(*mark("dve_mix", (l, "rinv", n)))
                dve.wait_ge(*at((l, "rinv", n)))
                ts(probs[0:qn, n % 2, 0:nk], probs[0:qn, n % 2, 0:nk], st[:, 3:4], None, ALU.mult, None, "dve_mix",
                   (l, "p", n))

            for n in range(len(items) + 1):
                if n < len(items):
                    hd, i = items[n]
                    q0, qn = TILES[i]
                    nk = q0 + qn
                    if i == 0:
                        dve.wait_ge(*at((l, "evac", TILE0["kn"] + 3)))
                    dve.wait_ge(*at((l, "s", n)))
                    b = 4 + 2 * (n % 2)
                    diag = flat(b, 256 + q0, qn)[0:qn]
                    tt(diag, diag, neg_qk[0:qn, 0:qn], ALU.add, "dve_mix", (l, "masked", n))
                    dve.wait_ge(*at((l, "masked", n)))
                    if n >= 2:
                        dve.wait_ge(*at((l, "rinv", n - 2)))
                    st = stat[0:qn, n % 2]
                    nc.vector.reduce_max(st[:, 0:1], flat(b, 256, nk)[0:qn], AX)\
                        .then_inc(*mark("dve_mix", (l, "max", n)))
                    dve.wait_ge(*at((l, "max", n)))
                    ts(st[:, 1:2], st[:, 0:1], -SC, None, ALU.mult, None, "dve_mix", (l, "nmax", n))
                if n >= 1:
                    normalise(n - 1)
            split_lo(1)
            branch(1)

            dve.wait_ge(*at(gy(l, 1, KD - 1)))
            nc.vector.memset(u_pad[:, :, 0:CV_W - 1], 0.0).then_inc(*mark("dve_mix", (l, "u_pad")))
            for i in range(4):
                t = TILE0["cv"] + 2 * i
                dve.wait_ge(*at((l, "tile", t)))
                dve.wait_ge(*at((l, "evac", t + 1)))
                tt(halves(u_pad[:, i, CV_W - 1:]), pair(tile0(l) + t), halves(gate_s[:, i % 2, :]), ALU.mult,
                   "dve_mix", (l, "evac", t))
            dve.wait_ge(*at((l, "evac", TILE0["cv"] + 6)))
            dve.wait_ge(*at((l, "u_pad")))
            for w in range(CV_W):
                for i in range(4):
                    src = u_pad[:, i, w:w + T]
                    label = (l, "cv_o", i) if w == CV_W - 1 else (l, "cvw", w, i)
                    if w == 0:
                        ts(cv_o[:, i, :], src, v("cvw", CV_W * i), v("cvb", i), ALU.mult, ALU.add, "dve_mix", label)
                    else:
                        dve.wait_ge(*at((l, "cvw", w - 1, i)))
                        stt(cv_o[:, i, :], src, v("cvw", CV_W * i + w), cv_o[:, i, :], ALU.mult, ALU.add, "dve_mix",
                            label)
            dve.wait_ge(*at((l, "cv_mu")))
            for i in range(4):
                dve.wait_ge(*at((l, "cv_o", i)))
                tt(cv_o[:, i, :], cv_o[:, i, :], gate_s[:, 0, :], ALU.subtract, "dve_mix", (l, "cv_c", i))
            dve.wait_ge(*at((l, "cv_rt")))
            nc.vector.reciprocal(gate_s[:, 1, :], gate_s[:, 1, :]).then_inc(*mark("dve_mix", (l, "cv_r")))
            dve.wait_ge(*at((l, "cv_r")))
            for i in range(4):
                stt(cv_o[:, i, :], cv_o[:, i, :], v("cvg", i), gate_s[:, 1, :], ALU.mult, ALU.mult, "dve_mix",
                    (l, "cv_n", i))
            split_lo(2)
            branch(2)
            for m in range(KD):
                dve.wait_ge(*at((l, "m_hi", m)))
                remainder(m_lo[:, m, :], acc[:, m, :], m_hi[:, m, :], "dve_mix", (l, "m", m))
            for m in range(KD):
                t = TILE0["mix"] + m
                dve.wait_ge(*at((l, "tile", t)))
                dve.wait_ge(*at((l, "m", m)))
                stt(halves(acc[:, m, :]), halves(h_hi[:, m, :].bitcast(F32)), ALPHA, pair(tile0(l) + t), ALU.mult,
                    ALU.add, "dve_mix", (l, "evac", t))
                dve.wait_ge(*at((l, "evac", t)))
                stt(acc[:, m, :], h_lo[:, m, :].bitcast(F32), ALPHA, acc[:, m, :], ALU.mult, ALU.add, "dve_ln",
                    (l, "ln1", "x", m))

            def norm(which, ready):
                dve.wait_ge(*at((l, which, "mu")))
                if which == "ln1":
                    dve.wait_ge(*at((l, "ln1", "x", KD - 1)))
                for k in range(KD):
                    tt(acc[:, k, :], acc[:, k, :], gate_s[:, 0, :], ALU.subtract, "dve_ln", (l, which, "c", k))
                dve.wait_ge(*at((l, which, "rt")))
                nc.vector.reciprocal(gate_s[:, 1, :], gate_s[:, 1, :]).then_inc(*mark("dve_ln", (l, which, "r")))
                dve.wait_ge(*at((l, which, "r")))
                for k in range(KD):
                    stt(acc[:, k, :], acc[:, k, :], v(which + "g", k), gate_s[:, 1, :], ALU.mult, ALU.mult, "dve_ln",
                        (l, which, "n", k))
                if which == "ln2" and l == DEPTH - 1:
                    return
                for k in range(KD):
                    dve.wait_ge(*at((l, which, "hi", k)))
                    remainder(h_lo[:, k, :], acc[:, k, :], h_hi[:, k, :], "dve_ln",
                              ready if k == KD - 1 else (l, which, "lo", k))

            norm("ln1", (l, "h_mid"))

            dve.wait_ge(*at((l, "h_mid")))
            for m in range(KD):
                ts(acc[:, m, :], h_hi[:, m, :].bitcast(F32), ALPHA, None, ALU.mult, None, "y_init", (l, "y0", m))
                dve.wait_ge(*at((l, "y0", m)))
                stt(acc[:, m, :], h_lo[:, m, :].bitcast(F32), ALPHA, acc[:, m, :], ALU.mult, ALU.add, "y_init",
                    (l, "y1", m))
            dve.wait_ge(*at((l, "y1", KD - 1)))
            e0 = EXP0[l]
            t0 = (l + 1) * MIX_TILES + EXP0[l] * PER_EXPERT
            g0 = (l + 1) * MIX_PANELS + EXP0[l] * PER_EXPERT
            if l == 1:
                dve.wait_ge(*at((l, "logits")))
                for c in range(NT):
                    nc.vector.max(top_v[:, c, :], logits[:, c, :]).then_inc(*mark("rt_dve", (l, "top", c)))
                    dve.wait_ge(*at((l, "top", c)))
                    nc.vector.max_index(top_i[:, c, :], top_v[:, c, :], logits[:, c, :])\
                        .then_inc(*mark("rt_dve", (l, "top_i", c)))
                dve.wait_ge(*at((l, "top_i", NT - 1)))
                nc.vector.tensor_copy(top_f[:], top_i[:, :, 0:2]).then_inc(*mark("rt_dve", (l, "top_f")))
                tt(top_w[:, :, 1:2], top_v[:, :, 1:2], top_v[:, :, 0:1], ALU.subtract, "rt_dve", (l, "w_arg"))
                dve.wait_ge(*at((l, "w_exp")))
                ts(top_v[:, :, 0:1], top_w[:, :, 1:2], 1.0, None, ALU.add, None, "rt_dve", (l, "w_sum"))
                dve.wait_ge(*at((l, "w_sum")))
                nc.vector.reciprocal(top_w[:, :, 0:1], top_v[:, :, 0:1]).then_inc(*mark("rt_dve", (l, "w0")))
                dve.wait_ge(*at((l, "w0")))
                tt(top_w[:, :, 1:2], top_w[:, :, 1:2], top_w[:, :, 0:1], ALU.mult, "rt_dve", (l, "w1"))
                dve.wait_ge(*at((l, "w1")))
                for j, dst in ((0, gates), (1, g_sel)):
                    tt(dst[:], bc(expert_no[:], 1, NT), bc(top_f[:, :, j], 2, N_EXP), ALU.is_equal, "rt_dve",
                       (l, "one_hot", j))
                    dve.wait_ge(*at((l, "one_hot", j)))
                    tt(dst[:], dst[:], bc(top_w[:, :, j], 2, N_EXP), ALU.mult, "rt_dve", (l, "weighted", j))
                    dve.wait_ge(*at((l, "weighted", j)))
                tt(gates[:], gates[:], g_sel[:], ALU.add, "rt_dve", (l, "gates"))
                dve.wait_ge(*at((l, "gates")))
            dve.wait_ge(lo_done, g0)

            def low(i2, n):
                cols = WIDE if n % PER_EXPERT < 2 * F_TILES else DEEP
                dve.wait_ge(hi_done, i2 * 60 + (g0 + n + 1))
                nc.vector.tensor_tensor(w_lo[:, n % 2, 0:cols], raw[:, n % RAW, 0:cols],
                                        w_hi[:, n % 2, 0:cols].bitcast(F32), ALU.subtract).then_inc(lo_done, 1)

            with nc.vector.Fori(0, EXPERTS[l] // 2) as i2:
                low(i2, 0)
                low(i2, 1)
                for x in range(2):
                    e = i2 * 2 + x
                    if l == 1:
                        dve.wait_ge(gb_pe, e + 1)
                        for c in range(NT):
                            src = gates[:, c, bass.ds(e, 1)].broadcast_to([P, P])
                            nc.vector.tensor_copy(gate_w[:, 0, c, :], src).then_inc(gb_copy, 1)
                        dve.wait_ge(gb_pe, e + 2)
                        nc.vector.tensor_copy(halves(gate_b[:, 0, :]), psum[:, 6:8, 0:HALF]).then_inc(gb_ready, 1)
                    for f in range(F_TILES):
                        n = x * PER_EXPERT + 2 * f
                        cnt = i2 * (2 * F_TILES) + ((e0 + x) * F_TILES + f)
                        low(i2, n + 2)
                        dve.wait_ge(silu_done, cnt + 2)
                        dve.wait_ge(tile_done, i2 * 60 + (t0 + n + 2))
                        if (e0 + x) * F_TILES + f >= 2:
                            dve.wait_ge(actl_done, cnt - 1)
                        nc.vector.tensor_tensor(halves(act_f[:, f % 2, :]), pair(1), halves(gate_s[:, f % 2, :]),
                                                ALU.mult).then_inc(act_done, 1)
                        low(i2, n + 3)
                        dve.wait_ge(acth_done, cnt + 1)
                        nc.vector.tensor_tensor(act_lo[:, f, :], act_f[:, f % 2, :], act_hi[:, f, :].bitcast(F32),
                                                ALU.subtract).then_inc(actl_done, 1)
                    for m in range(KD):
                        n = x * PER_EXPERT + 2 * F_TILES + m
                        dve.wait_ge(tile_done, i2 * 60 + (t0 + n + 1))
                        if l == 0:
                            nc.vector.tensor_tensor(halves(acc[:, m, :]), halves(acc[:, m, :]), pair(n), ALU.add)\
                                .then_inc(y_done, 1)
                        else:
                            nc.vector.tensor_tensor(halves(tmp_s[:, m % 2, :]), pair(n), halves(gate_b[:, 0, :]),
                                                    ALU.mult).then_inc(y_tmp, 1)
                            dve.wait_ge(y_tmp, i2 * (2 * KD) + (x * KD + m + 1))
                            nc.vector.tensor_tensor(acc[:, m, :], acc[:, m, :], tmp_s[:, m % 2, :], ALU.add)\
                                .then_inc(y_done, 1)
                        if n + 2 < 60:
                            low(i2, n + 2)
            dve.wait_ge(y_done, 1 + (e0 + EXPERTS[l]) * KD)
            norm("ln2", (l + 1, "h"))


def blocks(w, cols):
    w = w[:, cols]
    return np.ascontiguousarray(w.reshape(-1, P, len(cols)).transpose(1, 0, 2)).reshape(P, -1)


def mixer_panels(w_in, w_uq, w_ukv, w_br, w_out):
    sizes = (256, 128, 32, 1536, 512, 4, 4, 512, 512, D, D, D)
    cq, ckv, kr, dn, z, b, _, cva, cvb, *gate = np.concatenate([[0], np.cumsum(sizes)])[:-1].tolist()
    tile = lambda c0, i: np.arange(c0 + P * i, c0 + P * (i + 1))
    out = [blocks(w_in, tile(dn, i)) for i in range(12)]
    small = np.zeros((P, WIDE), w_in.dtype)
    small[:, 0:8 * KD] = blocks(w_in, np.arange(b, b + 8))
    out.append(small)
    out += [blocks(w_in, tile(z, i)) for i in range(4)]

    def branch(n):
        w = w_br[n]
        got = []
        for i in range(4):
            got += [blocks(w_in, tile(gate[(1, 0, 2)[n]], 2 * i + j)) for j in range(2)]
            got.append(np.concatenate([blocks(w, tile(0, 2 * i + j)) for j in range(2)], 1))
        return got

    out += branch(0)
    out += [blocks(w_in, tile(cq, i)) for i in range(2)] + [blocks(w_in, tile(ckv, 0))]
    turned = np.concatenate([np.arange(ROPE // 2, ROPE), np.arange(ROPE // 2)])
    out.append(blocks(w_in, np.concatenate([np.arange(kr - NOPE, kr + ROPE), kr + turned])))
    for half in range(2):
        out.append(np.concatenate([blocks(w_uq, np.concatenate([np.arange(QK * hd, QK * (hd + 1)),
                                                               QK * hd + NOPE + turned]))
                                   for hd in range(4 * half, 4 * half + 4)], 1))
    part = lambda hd, c0: np.arange(hd * (NOPE + VD) + c0, hd * (NOPE + VD) + c0 + 64)
    out.append(np.concatenate([blocks(w_ukv, np.concatenate([part(2 * i, c0), part(2 * i + 1, c0)]))
                               for c0 in (0, NOPE) for i in range(4)], 1))
    out += branch(1)
    for i in range(4):
        out += [blocks(w_in, tile(cva, i)), blocks(w_in, tile(cvb, i))]
    out += branch(2)
    out += [blocks(w_out, tile(0, i)) for i in range(8)]
    assert len(out) == MIX_PANELS
    return np.stack(out)


def columns(x):
    return x.reshape(-1, P).T


def host_arrays(a):
    f = np.float32
    got = {}
    h0 = np.concatenate([a["meta_tokens"], a["x"][0]], 0)
    got["h0"] = np.ascontiguousarray(h0.T.reshape(KD, P, T).transpose(1, 0, 2))
    got["mix_panels"] = np.stack([
        mixer_panels(a["w_in"][l], a["mla_w_uq"][l], a["mla_w_ukv"][l],
                     (a["w_br_dn"][l], a["w_br_mla"][l], a["w_br_cv"][l]), a["w_mix_out"][l]) for l in range(DEPTH)])
    FE = F_TILES * P
    experts = [tuple(w[0][:, x * FE:(x + 1) * FE] for w in (a["ffn_w_gate"], a["ffn_w_up"]))
               + (a["ffn_w_down"][0][x * FE:(x + 1) * FE],) for x in range(EXPERTS[0])]
    experts += [tuple(w[0][e] for w in (a["moe_w_gate"], a["moe_w_up"], a["moe_w_down"])) for e in range(N_EXP)]
    tile = lambda i: np.arange(P * i, P * (i + 1))
    got["up_panels"] = np.stack([np.stack([blocks(w, tile(i)) for i in range(F_TILES) for w in (wg, wu)])
                                 for wg, wu, _ in experts])
    got["down_panels"] = np.stack([np.stack([blocks(wd, tile(i)) for i in range(KD)]) for _, _, wd in experts])
    vecs = []
    for l in range(DEPTH):
        conv = a["dn_conv_w"][l].reshape(4, 12, P).transpose(2, 1, 0).reshape(P, -1)
        cvw = a["cv_dw_w"][l].reshape(CV_W, 4, P).transpose(2, 1, 0).reshape(P, -1)
        row = lambda x: np.broadcast_to(x[None, :], (P, x.shape[0]))
        vecs.append(np.concatenate([
            columns(a["mla_q_norm"][l]), columns(a["mla_kv_norm"][l]), conv, columns(a["dn_o_norm"][l]), cvw,
            columns(a["cv_dw_b"][l]), columns(a["cv_ln_g"][l]), columns(a["cv_ln_b"][l]), columns(a["ln1_g"][l]),
            columns(a["ln1_b"][l]), columns(a["ln2_g"][l]), columns(a["ln2_b"][l]), row(a["dn_a_log"][l]),
            row(a["dn_dt_bias"][l])], 1))
    got["vec"] = np.stack(vecs)
    got["router"] = blocks(a["moe_w_router"][0], np.arange(N_EXP)).reshape(P, KD, N_EXP)
    i, j = np.arange(P)[None, :], np.arange(P)[:, None]
    got["ident"] = (i == j).astype(f)
    got["cum_mask"] = (j <= i).astype(f)
    got["neg_ji"] = np.where(i < j, f(NEG), f(0))
    got["neg_qk"] = np.where(i > j, f(NEG), f(0))
    got["level_mask"] = np.stack([((j >> b) % 2 == 1) & ((i >> b) == (j >> b) - 1) for b in range(LEVELS)], 1)\
        .astype(f)
    meta = np.ones((P, NT, DN_H), f)
    meta[N_META:, 0, :] = 0
    got["meta_rows"] = meta
    inv = f(10000.0) ** (-np.arange(0, ROPE, 2, dtype=f) / f(ROPE))
    ang = (np.arange(T, dtype=f)[:, None] * inv[None, :]).T
    rope = np.zeros((P, T), f)
    rope[NOPE:QK] = np.concatenate([np.cos(ang), np.cos(ang)])
    rope[QK:P] = np.concatenate([-np.sin(ang), np.sin(ang)])
    got["rope"] = rope
    got["expert_no"] = np.broadcast_to(np.arange(N_EXP, dtype=f)[None, :], (P, N_EXP))
    return {f"in_{k}": np.ascontiguousarray(v) for k, v in got.items()}


def kernel(**inputs):
    import concourse.bacc as bacc
    from concourse.bass_utils import run_bass_kernel_spmd

    arrays = host_arrays({k: np.asarray(x) for k, x in inputs.items()})
    notes = None
    for _ in range(2):
        nc = bacc.Bacc("TRN2", target_bir_lowering=False, num_devices=1)
        ins = {k[3:]: nc.dram_tensor(k, x.shape, mybir.dt.from_np(x.dtype), kind="ExternalInput").ap()
               for k, x in arrays.items()}
        out = nc.dram_tensor("out", (P, KD, SEQ), F32, kind="ExternalOutput").ap()
        counts = Counts(notes)
        program(nc, counts, ins, out)
        notes = counts.notes
    r = run_bass_kernel_spmd(nc, [arrays], core_ids=[0])
    got = r.results[0]["out"]
    return np.ascontiguousarray(got.transpose(1, 0, 2)).reshape(D, SEQ).T[None]
```

```python
from contextlib import ExitStack

import numpy as np

import concourse.bass as bass
import concourse.mybir as mybir
from concourse.alu_op_type import AluOpType as ALU

F32 = mybir.dt.float32
F32R = mybir.dt.float32r
U32 = mybir.dt.uint32
I32 = mybir.dt.int32
ACT = mybir.ActivationFunctionType
AX = mybir.AxisListType.X

P = 128
D = 1024
KD = D // P
N_META, SEQ = 16, 512
T = N_META + SEQ
HALF = T // 2
DEPTH = 2
HEADS, NOPE, ROPE, VD = 8, 64, 32, 64
QK = NOPE + ROPE
DN_H = 4
CV_W = 31
ALPHA = (2 * DEPTH) ** 0.25
EPS = 1e-6
NEG = -1e30
N_EXP = 8
F_TILES = 11
CAP = 192
CT = CAP // 2
ROUNDS = -(-SEQ // CAP)
TILES = [(0, N_META)] + [(N_META + P * i, P) for i in range(SEQ // P)]
NT = len(TILES)
WIN = [s for s, _ in TILES]
LEVELS = 7

MIX_PANELS = 76
MIX_TILES = 102
RAW = 4
AHEAD = 4
WIDE, DEEP = KD * P, F_TILES * P
EXPERTS = (2, N_EXP)
PER_EXPERT = 2 * F_TILES + KD

SEGMENTS = [("qkv", 12), ("ba", 1), ("g0", 8), ("z", 4), ("c", 4), ("p0", 8), ("uq", 8), ("kn", 4), ("v", NT),
            ("cv", 8), ("g1", 8), ("g2", 8), ("p1", 8), ("p2", 8), ("mix", 8)]
TILE0, _n = {}, 0
for _name, _k in SEGMENTS:
    TILE0[_name] = _n
    _n += _k
assert _n == MIX_TILES
PANEL0, LAST_TILE = {}, []
for _name, _k in SEGMENTS:
    PANEL0[_name] = len(LAST_TILE)
    if _name[0] == "p":
        LAST_TILE += [TILE0[_name] + 2 * i + 1 for i in range(4)]
    elif _name == "uq":
        LAST_TILE += [TILE0[_name] + 3, TILE0[_name] + 7]
    elif _name == "v":
        LAST_TILE.append(TILE0["v"] + NT - 1)
    elif _name != "kn":
        LAST_TILE += [TILE0[_name] + i for i in range(_k)]
assert len(LAST_TILE) == MIX_PANELS

VEC = {}
_n = 0
for _name, _k in (("q_norm", 2), ("kv_norm", 1), ("conv", 12 * 4), ("o_norm", 1), ("cvw", 4 * CV_W), ("cvb", 4),
                  ("cvg", 4), ("cvlb", 4), ("ln1g", 8), ("ln1b", 8), ("ln2g", 8), ("ln2b", 8),
                  ("a_log", 4), ("dt", 4)):
    VEC[_name] = _n
    _n += _k
NVEC = _n


class Counts:

    def __init__(self, notes=None):
        self.first = notes is None
        self.notes = {} if notes is None else notes
        self.raised = {}
        self.sems = {}

    def mark(self, name, label, n=1):
        self.raised[name] = self.raised.get(name, 0) + n
        if self.first:
            assert label not in self.notes, label
            self.notes[label] = (name, self.raised[name])
        return self.sems[name], n

    def at(self, label):
        if self.first and label not in self.notes:
            return next(iter(self.sems.values())), 1
        name, value = self.notes[label]
        return self.sems[name], value


def program(nc, counts, ins, out):
    mark, at = counts.mark, counts.at
    with ExitStack() as ctx:
        _program(nc, ctx, counts, mark, at, ins, out)


def _program(nc, ctx, counts, mark, at, ins, out):
    def sb(name, shape, dt=F32, where=None):
        return (where or ctx).enter_context(nc.sbuf_tensor(name, shape, dt))

    def sem(name):
        s = ctx.enter_context(nc.semaphore(name))
        counts.sems[name] = s
        return s

    h_hi = sb("h_hi", [P, KD, T], F32R)
    h_lo = sb("h_lo", [P, KD, T], F32R)
    raw = sb("raw", [P, RAW, DEEP])
    w_hi = sb("w_hi", [P, 2, DEEP], F32R)
    w_lo = sb("w_lo", [P, 2, DEEP], F32R)
    ident = sb("ident", [P, P])
    ones = sb("ones", [P, P])
    cum_mask = sb("cum_mask", [P, P])
    neg_ji = sb("neg_ji", [P, P])
    neg_qk = sb("neg_qk", [P, P])
    level_mask = sb("level_mask", [P, LEVELS, P])
    meta_rows = sb("meta_rows", [P, NT, DN_H])
    rope = sb("rope", [P, T])
    expert_no = sb("expert_no", [P, N_EXP])
    eps = sb("eps", [P, 1])
    vec = sb("vec", [P, NVEC])
    router = sb("router", [P, KD, N_EXP])
    router_hi = sb("router_hi", [P, KD, N_EXP], F32R)
    router_lo = sb("router_lo", [P, KD, N_EXP], F32R)
    acc = sb("acc", [P, KD, T])
    z_ph = ExitStack()
    z_s = sb("z_s", [P, 4, T], where=z_ph)
    z_ph.close()
    br_hi = sb("br_hi", [P, 4, T], F32R)
    br_lo = sb("br_lo", [P, 4, T], F32R)
    gate_s = sb("gate_s", [P, 2, T])
    tmp_s = sb("tmp_s", [P, 2, T])

    ph = ExitStack()
    qkv = sb("qkv", [P, 12, T], where=ph)
    ba = sb("ba", [P, NT, 8], where=ph)
    g_tok = sb("g_tok", [P, NT, DN_H], where=ph)
    b_tok = sb("b_tok", [P, NT, DN_H], where=ph)
    sp1 = sb("sp1", [P, NT, DN_H], where=ph)
    sp2 = sb("sp2", [P, NT, DN_H], where=ph)
    ea = sb("ea", [P, DN_H], where=ph)
    cums = sb("cums", [P, NT, 2 * DN_H], where=ph)
    ecum = sb("ecum", [P, NT, 2 * DN_H], where=ph)
    eneg = sb("eneg", [P, NT, DN_H], where=ph)
    conv_ph = ExitStack()
    x_pad = sb("x_pad", [P, 2, 3 + T], where=conv_ph)
    conv_o = sb("conv_o", [P, 2, T], where=conv_ph)
    conv_ph.close()
    GRP = 3
    wk = sb("wk", [P, 2, 4, P], where=ph)
    dT = sb("dT", [P, GRP, 4, P], where=ph)
    dN = sb("dN", [P, GRP, 4, P], where=ph)
    aN = sb("aN", [P, GRP, 4, P], where=ph)
    lvl_e = sb("lvl_e", [P, 3, 4, P], where=ph)
    lvl_x = sb("lvl_x", [P, 3, 4, P], where=ph)
    qkg = sb("qkg", [P, GRP, 4, P], where=ph)
    kdec = sb("kdec", [P, GRP, 4, P], where=ph)
    vtok = sb("vtok", [P, GRP, 4, P], where=ph)
    state = sb("state", [P, 4, P], where=ph)
    ph.close()
    ph = ExitStack()
    qT = sb("qT", [P, HEADS, T], where=ph)
    c_f = sb("c_f", [P, 3, T], where=ph)
    cn_hi = sb("cn_hi", [P, 3, T], F32R, where=ph)
    cn_lo = sb("cn_lo", [P, 3, T], F32R, where=ph)
    kT = sb("kT", [P, HEADS, T], where=ph)
    v_tok = sb("v_tok", [P, NT, HEADS * VD], where=ph)
    att_o = sb("att_o", [P, 4, T], where=ph)
    probs = sb("probs", [P, 2, T], where=ph)
    probsT = sb("probsT", [P, 2, NT, P], where=ph)
    stat = sb("stat", [P, 3, 4], where=ph)
    ph.close()
    ph = ExitStack()
    u_pad = sb("u_pad", [P, 4, CV_W - 1 + T], where=ph)
    cv_o = sb("cv_o", [P, 4, T], where=ph)
    m_lo = sb("m_lo", [P, KD, T], F32R, where=ph)
    gate2 = sb("gate2", [P, KD, T], where=ph)
    gate1_ph = ExitStack()
    gate1 = sb("gate1", [P, KD, T], where=gate1_ph)
    gate1_ph.close()
    m_hi = sb("m_hi", [P, KD, T], F32R, where=ph)
    ph.close()
    ph = ExitStack()
    act_f = sb("act_f", [P, 2, T], where=ph)
    act_hi = sb("act_hi", [P, F_TILES, T], F32R, where=ph)
    act_lo = sb("act_lo", [P, F_TILES, T], F32R, where=ph)
    more_w = sb("more_w", [P, 2, 2, DEEP], F32R, where=ph)
    ph.close()
    ph = ExitStack()
    column_no = sb("column_no", [P, CAP], where=ph)
    logits = sb("logits", [P, NT, N_EXP], where=ph)
    gates = sb("gates", [P, NT, N_EXP], where=ph)
    chosen = sb("chosen", [P, NT, N_EXP], where=ph)
    g_sel = sb("g_sel", [P, NT, N_EXP], where=ph)
    slots = sb("slots", [P, 4, N_EXP + 1], where=ph)
    top_v = sb("top_v", [P, NT, 8], where=ph)
    top_i = sb("top_i", [P, NT, 8], U32, where=ph)
    top_f = sb("top_f", [P, NT, 2], where=ph)
    top_w = sb("top_w", [P, NT, 2], where=ph)
    load_max = sb("load_max", [P, 4], where=ph)
    rounds_i = sb("rounds_i", [P, 1], I32, where=ph)
    tok_hi = sb("tok_hi", [P, 4, D], F32R, where=ph)
    tok_lo = sb("tok_lo", [P, 4, D], F32R, where=ph)
    xc = sb("xc", [P, KD, 2, CAP], F32R, where=ph)
    pick = sb("pick", [P, 2, 4, CAP], F32R, where=ph)
    put = sb("put", [CT, 2, SEQ], F32R, where=ph)
    moe_g = sb("moe_g", [P, 2, CAP], where=ph)
    moe_a = sb("moe_a", [P, 2, CAP], where=ph)
    ma = sb("ma", [P, F_TILES, 2, CAP], F32R, where=ph)
    y_f = sb("y_f", [P, 2, CAP], where=ph)
    gate_c = sb("gate_c", [CT, 2], where=ph)
    ph.close()
    yt_hi, yt_lo = (x[0:CT].rearrange("p a t -> p (a t)")[:, 0:2 * D].rearrange("p (c d) -> p c d", c=2)
                    for x in (br_hi, br_lo))

    more_w1 = [x[:].rearrange("p a t -> p (a t)")[:, 0:2 * DEEP].rearrange("p (a n) -> p a n", a=2)
               for x in (h_hi, h_lo)]

    def ffn_w(l, n, part):
        if n % 4 < 2:
            return (w_hi, w_lo)[part][:, n % 4, :]
        return more_w[:, n % 4 - 2, part, :] if l == 0 else more_w1[n % 4 - 2][:, part, :]

    psum = ctx.enter_context(nc.psum_tensor("psum", [P, 8, 512], F32))

    def pair(t):
        return psum[:, 2 * (t % 2):2 * (t % 2) + 2, 0:HALF]

    def halves(ap):
        return ap.rearrange("p (h n) -> p h n", h=2)

    def work2(i):
        return psum[:, 4 + 2 * (i % 2):6 + 2 * (i % 2), 0:HALF]

    def bank4(b):
        return psum[:, b, :].rearrange("p (h n) -> p h n", h=4)

    def flat(b0, c0, n):
        return psum[:, b0:8, :].rearrange("p b n -> p (b n)")[:, c0:c0 + n]

    def vcol(name, i=0, rows=slice(0, P)):
        return vec[rows, VEC[name] + i:VEC[name] + i + 1]

    def bc(ap, axis, n):
        ap = ap.unsqueeze(axis)
        shape = list(ap.shape)
        shape[axis] = n
        return ap.broadcast_to(shape)

    def gate_of(n, m):
        return (acc, gate1, gate2)[n][:, m, :]

    def branch_src(n):
        return (qkv, att_o, cv_o)[n]

    raw_in = [sem(f"raw_in{j}") for j in range(RAW)]
    h_in = [sem(f"h_in{j}") for j in range(4)]
    const_in = sem("const_in")
    vec_in = sem("vec_in")
    set_up = sem("set_up")
    hi_done = sem("hi_done")
    lo_done = [sem("lo_even"), sem("lo_odd")]
    tile_done = sem("tile_done")
    act_mix = sem("act_mix")
    dve_mix = sem("dve_mix")
    pool_mix = sem("pool_mix")
    pe_mix = sem("pe_mix")
    act_ln = sem("act_ln")
    dve_ln = sem("dve_ln")
    pe_ln = sem("pe_ln")
    silu_done = sem("silu_done")
    act_done = sem("act_done")
    acth_done = sem("acth_done")
    actl_done = sem("actl_done")
    y_done = sem("y_done")
    y_init = sem("y_init")
    rt_pe, rt_act, rt_dve = sem("rt_pe"), sem("rt_act"), sem("rt_dve")
    m_pick = sem("m_pick")
    m_gather = sem("m_gather")
    m_x = sem("m_x")
    m_gsum, m_usum = sem("m_gsum"), sem("m_usum")
    m_silu = sem("m_silu")
    m_act = sem("m_act")
    ma_h, ma_l = sem("ma_h"), sem("ma_l")
    m_turn = sem("m_turn")
    m_put = sem("m_put")
    m_y = sem("m_y")
    m_yt = sem("m_yt")
    m_yhi, m_ylo = sem("m_yhi"), sem("m_ylo")
    m_scat = sem("m_scat")
    m_shift = sem("m_shift")
    m_add = sem("m_add")
    out_done = sem("out_done")

    def gy(l, n, m):
        return l, "evac", TILE0[f"p{n}"] + m

    EXP0 = [0, EXPERTS[0]]

    def panel0(l):
        return l * MIX_PANELS + EXP0[l] * PER_EXPERT

    def tile0(l):
        return l * MIX_TILES + EXP0[l] * PER_EXPERT

    block = ctx.enter_context(nc.Block())

    def rounds_of(eng):
        eng.wait_ge(*at("rounds"))
        return eng.value_load(rounds_i[0:1, 0:1], min_val=1, max_val=ROUNDS)

    @block.sync
    def _(sp):
        def first_panel(j):
            sp.dma_start(raw[:, j, 0:WIDE], ins["mix_panels"][0, j]).then_inc(raw_in[j], 16)

        first_panel(0)
        for j in range(4):
            sp.dma_start(acc[:, 2 * j:2 * j + 2, :], ins["h0"][:, 2 * j:2 * j + 2, :]).then_inc(h_in[j], 16)
        first_panel(1)
        sp.dma_start(vec[:], ins["vec"][0]).then_inc(vec_in, 16)
        first_panel(2)
        for name, dst in (("ident", ident), ("cum_mask", cum_mask), ("neg_ji", neg_ji), ("neg_qk", neg_qk),
                          ("level_mask", level_mask), ("meta_rows", meta_rows), ("rope", rope),
                          ("expert_no", expert_no), ("router", router)):
            sp.dma_start(dst[:], ins[name]).then_inc(const_in, 16)
        first_panel(3)

        def load(slot, src, cols, par, count):
            sp.wait_ge(lo_done[par], count)
            sp.dma_start(raw[:, slot, 0:cols], src).then_inc(raw_in[slot], 16)

        for l in range(DEPTH):
            g0 = panel0(l)
            with nc.sync.Fori(0, MIX_PANELS // RAW - (l == 0)) as i:
                for j in range(RAW):
                    q = i * RAW + j + (RAW if l == 0 else 0)
                    src = ins["mix_panels"][l, bass.ds(q, 1)].rearrange("a p n -> p (a n)")
                    first = g0 + j - (RAW if l else 0)
                    load(j, src, WIDE, first % 2, i * (RAW // 2) + (first // 2 + 1))
            g0 += MIX_PANELS

            def expert_panel(n, i, before):
                f = n % PER_EXPERT
                e = i * 2 + (EXP0[l] + n // PER_EXPERT)
                name, j, cols = ("up_panels", f, WIDE) if f < 2 * F_TILES else ("down_panels", f - 2 * F_TILES, DEEP)
                src = ins[name][e, j] if isinstance(e, int) else \
                    ins[name][bass.ds(e, 1), j].rearrange("a p n -> p (a n)")
                load(n % RAW, src, cols, n % 2, before + ((g0 + n - RAW) // 2 + 1))

            for n in range(2 * PER_EXPERT if l == 0 else AHEAD):
                expert_panel(n, 0, 0)
            if l == 1:
                rounds = rounds_of(sp)
                with nc.sync.Fori(0, rounds) as r:
                    with nc.sync.Fori(0, N_EXP // 2) as i:
                        for n in range(AHEAD, 2 * PER_EXPERT + AHEAD):
                            expert_panel(n, i, r * (N_EXP * PER_EXPERT // 2) + i * PER_EXPERT)
        for c in range(KD):
            sp.wait_ge(*at((DEPTH - 1, "ln2", "out", c)))
            sp.dma_start(out[:, c, :], acc[:, c, N_META:T]).then_inc(out_done, 16)
        sp.wait_ge(out_done, 16 * KD)

    @block.gpsimd
    def _(pool):
        nc.gpsimd.memset(ones[:], 1.0).then_inc(*mark("set_up", "ones"))
        nc.gpsimd.memset(eps[:], EPS).then_inc(*mark("set_up", "eps"))
        for l in range(DEPTH):
            for p in range(MIX_PANELS):
                g = panel0(l) + p
                pool.wait_ge(hi_done, g + 1)
                nc.gpsimd.tensor_tensor(w_lo[:, g % 2, 0:WIDE], raw[:, g % RAW, 0:WIDE],
                                        w_hi[:, g % 2, 0:WIDE].bitcast(F32), ALU.subtract).then_inc(lo_done[g % 2], 1)
                if p >= PANEL0["cv"] + 3 and (p - PANEL0["cv"]) % 2 and p < PANEL0["cv"] + 11:
                    i = (p - PANEL0["cv"] - 3) // 2
                    pool.wait_ge(*at((l, "evac", TILE0["cv"] + 2 * i)))
                    pool.wait_ge(*at((l, "evac", TILE0["cv"] + 2 * i + 1)))
                    nc.gpsimd.tensor_tensor(u_pad[:, i, CV_W - 1:], u_pad[:, i, CV_W - 1:], cv_o[:, i, :], ALU.mult)\
                        .then_inc(*mark("pool_mix", (l, "glu", i)))

            g0 = panel0(l) + MIX_PANELS

            def low(n, before):
                cols = WIDE if n % PER_EXPERT < 2 * F_TILES else DEEP
                pool.wait_ge(hi_done, before + (g0 + n + 1))
                nc.gpsimd.tensor_tensor(ffn_w(l, n, 1)[:, 0:cols], raw[:, n % RAW, 0:cols],
                                        ffn_w(l, n, 0)[:, 0:cols].bitcast(F32), ALU.subtract).then_inc(lo_done[0], 1)

            if l == 0:
                for n in range(0, 2 * PER_EXPERT, 2):
                    low(n, 0)
            else:
                for n in range(0, AHEAD, 2):
                    low(n, 0)
                rounds = rounds_of(pool)
                with nc.gpsimd.Fori(0, rounds) as r:
                    with nc.gpsimd.Fori(0, N_EXP // 2) as i:
                        for n in range(AHEAD, 2 * PER_EXPERT + AHEAD, 2):
                            low(n, r * (N_EXP * PER_EXPERT) + i * (2 * PER_EXPERT))

    @block.tensor
    def _(pe):
        for s_ in (m_gather, m_scat, m_turn, m_yt):
            pe.sem_inc(s_, 1)
        last_read = {}

        def take(banks, *readers):
            waits = {}
            for b in banks:
                for label in last_read.get(b, ()):
                    s, n = at(label)
                    waits[id(s)] = (s, max(n, waits.get(id(s), (s, 0))[1]))
                last_read[b] = readers
            for s, n in waits.values():
                pe.wait_ge(s, n)

        def mm3(dst, w_h, w_l, x_h, x_l, start, stop):
            nc.tensor.matmul(dst, w_h, x_h, start=start, stop=False)
            nc.tensor.matmul(dst, w_l, x_h, start=False, stop=False)
            return nc.tensor.matmul(dst, w_h, x_l, start=False, stop=stop)

        def product(dst, w_h, w_l, b0, nb, x_h, x_l, ready=None):
            for k in range(nb):
                if ready:
                    ready(k)
                cols = slice((b0 + k) * P, (b0 + k + 1) * P)
                for hf in range(2):
                    tok = slice(hf * HALF, (hf + 1) * HALF)
                    last = mm3(dst[:, hf, :], w_h[:, cols], w_l[:, cols], x_h[:, k, tok], x_l[:, k, tok],
                               k == 0, k == nb - 1)
            return last

        def sum_rows(dst, src, start, stop):
            for hf in range(2):
                last = nc.tensor.matmul(dst[:, hf, :], ones[:], src[:, hf * HALF:(hf + 1) * HALF],
                                        start=start, stop=stop)
            return last

        def tile_of(l, name, i, b0, nb, x_h, x_l, panel, ready=None, last_banks=False):
            t = TILE0[name] + i
            g = panel0(l) + panel
            pe.wait_ge(lo_done[g % 2], g // 2 + 1)
            bt = 3 if last_banks else (tile0(l) + t) % 2
            take((2 * bt, 2 * bt + 1), (l, "evac", t))
            product(work2(1) if last_banks else pair(bt), w_hi[:, g % 2], w_lo[:, g % 2], b0, nb, x_h, x_l, ready).then_inc(*mark("tile_done", (l, "tile", t)))

        def turn_y(pe, v, m):
            pe.wait_ge(m_y, v * KD + m + 2)
            if m % 4 == 0:
                pe.wait_ge(m_ylo, v * 4 + (2 * (m // 4) + 1))
                pe.wait_ge(m_put, v * 3 + 4)
            for ct in range(2):
                last = nc.tensor.transpose(psum[0:CT, 2 + ct, (m % 4) * P:(m % 4 + 1) * P],
                                           y_f[:, m % 2, ct * CT:(ct + 1) * CT], ident[:])
            last.then_inc(m_yt, 1)

        def gates_tile(l, n, m):
            tile_of(l, f"g{n}", m, 0, KD, h_hi, h_lo, PANEL0[f"g{n}"] + m)

        def proj_tile(l, n, m):
            if m == 0:
                pe.wait_ge(*at((l, "br", n)))
            tile_of(l, f"p{n}", m, 4 * (m % 2), 4, br_hi, br_lo, PANEL0[f"p{n}"] + m // 2)

        for l in range(DEPTH):
            for i in range(12):
                tile_of(l, "qkv", i, 0, KD, h_hi, h_lo, i, (lambda k: pe.wait_ge(*at((l, "h", k)))) if i == 0 else None)
            t = TILE0["ba"]
            bt = (tile0(l) + t) % 2
            pe.wait_ge(lo_done[0], panel0(l) // 2 + 7)
            take((2 * bt, 2 * bt + 1), (l, "evac", t))
            s = (panel0(l) + 12) % 2
            for c in range(NT):
                for k in range(KD):
                    last = mm3(psum[:, 2 * bt, 8 * c:8 * c + 8], h_hi[:, k, WIN[c]:WIN[c] + P],
                               h_lo[:, k, WIN[c]:WIN[c] + P], w_hi[:, s, 8 * k:8 * k + 8],
                               w_lo[:, s, 8 * k:8 * k + 8], k == 0, k == KD - 1)
            last.then_inc(*mark("tile_done", (l, "tile", t)))
            for i in range(8):
                pe.wait_ge(*at((l, "qk_sq", i)))
                take((4 + 2 * (i % 2), 5 + 2 * (i % 2)), (l, "qk_rt", i))
                sum_rows(work2(i), tmp_s[:, i % 2, :], True, True).then_inc(*mark("pe_mix", (l, "qk_ss", i)))
                gates_tile(l, 0, i)

            def chunk_setup(c, b):
                w = slice(WIN[c], WIN[c] + P)
                pe.wait_ge(*at((l, "gb", c)))
                take((4,), (l, "cum_s", c))
                nc.tensor.matmul(psum[:, 4, 0:4], cum_mask[:], g_tok[:, c, :], start=True, stop=True)
                nc.tensor.matmul(psum[:, 4, 4:8], ones[:], g_tok[:, c, :], start=True, stop=True)\
                    .then_inc(*mark("pe_mix", (l, "cum", c)))
                take((5,), (l, "diff", c), (l, "eB", c))
                for hd in range(4):
                    last = nc.tensor.matmul(bank4(5)[:, hd, :], wk[:, 0, hd, :], cum_mask[:], start=True, stop=True)
                last.then_inc(*mark("pe_mix", (l, "cumB", c)))
                take((3,), (l, "m1", c))
                for hd in range(4):
                    kk = qkv[:, 4 + hd, w]
                    last = nc.tensor.matmul(bank4(3)[:, hd, :], kk, kk, start=True, stop=True)
                last.then_inc(*mark("pe_mix", (l, "kk", c)))
                take((4,), (l, "qkg", c))
                for hd in range(4):
                    last = nc.tensor.matmul(bank4(4)[:, hd, :], qkv[:, 4 + hd, w], qkv[:, hd, w], start=True, stop=True)
                last.then_inc(*mark("pe_mix", (l, "qk", c)))
                take((0,), (l, "kdec", c))
                for hd in range(4):
                    last = nc.tensor.transpose(bank4(0)[:, hd, :], qkv[:, 4 + hd, w], ident[:])
                last.then_inc(*mark("pe_mix", (l, "ktok", c)))
                take((1,), (l, "vtok", c))
                for hd in range(4):
                    last = nc.tensor.transpose(bank4(1)[:, hd, :], qkv[:, 8 + hd, w], ident[:])
                last.then_inc(*mark("pe_mix", (l, "vtr", c)))
                if c < 4:
                    tile_of(l, "z", c, 0, KD, h_hi, h_lo, PANEL0["z"] + c, last_banks=True)
                pe.wait_ge(*at((l, "m1", c)))
                take((2,), (l, "aN", c))
                for hd in range(4):
                    last = nc.tensor.transpose(bank4(2)[:, hd, :], wk[:, 1, hd, :], ident[:])
                last.then_inc(*mark("pe_mix", (l, "aT", c)))

            def level(c, b, lv, n):
                x_b = n % 3
                pe.wait_ge(*at((l, "E", c, lv)))
                if lv:
                    pe.wait_ge(*at((l, "dN", c, lv - 1)))
                    pe.wait_ge(*at((l, "dT", c, lv - 1)))
                take((x_b,), (l, "X", c, lv))
                for hd in range(4):
                    last = nc.tensor.matmul(bank4(x_b)[:, hd, :], lvl_e[:, n % 3, hd, :],
                                            dT[:, b, hd, :] if lv else ident[:], start=True, stop=True)
                last.then_inc(*mark("pe_mix", (l, "Xp", c, lv)))

            def level_y(c, b, lv, n):
                y_b = 3 + n % 3
                pe.wait_ge(*at((l, "X", c, lv)))
                take((y_b,), (l, "dT", c, lv))
                for hd in range(4):
                    last = nc.tensor.matmul(bank4(y_b)[:, hd, :], dN[:, b, hd, :] if lv else ident[:],
                                            lvl_x[:, n % 3, hd, :], start=True, stop=True)
                last.then_inc(*mark("pe_mix", (l, "Yp", c, lv)))

            def level_t(c, b, lv, n):
                t_b = n % 3
                pe.wait_ge(*at((l, "dT", c, lv)))
                take((t_b,), (l, "dN", c, lv))
                for hd in range(4):
                    last = nc.tensor.transpose(bank4(t_b)[:, hd, :], dT[:, b, hd, :], ident[:])
                last.then_inc(*mark("pe_mix", (l, "Tp", c, lv)))

            def recur(c, b):
                s0, n = TILES[c]
                w = slice(WIN[c], WIN[c] + P)
                pe.wait_ge(*at((l, "ds", c - 1) if c else (l, "state0")))
                take((0,), (l, "r1", c))
                for hd in range(4):
                    last = nc.tensor.matmul(bank4(0)[:, hd, :], qkv[:, 4 + hd, w], state[:, hd, :],
                                            start=True, stop=True)
                last.then_inc(*mark("pe_mix", (l, "ks", c)))
                pe.wait_ge(*at((l, "R", c)))
                pe.wait_ge(*at((l, "TT", c)))
                take((1,), (l, "u", c))
                for hd in range(4):
                    last = nc.tensor.matmul(bank4(1)[:, hd, :], dT[:, b, hd, :], lvl_e[:, 0, hd, :],
                                            start=True, stop=True)
                last.then_inc(*mark("pe_mix", (l, "up", c)))
                pe.wait_ge(*at((l, "u", c)))
                take((3,), (l, "ds", c))
                for hd in range(4):
                    last = nc.tensor.matmul(bank4(3)[:, hd, :], kdec[:, b, hd, :], lvl_x[:, 0, hd, :],
                                            start=True, stop=True)
                last.then_inc(*mark("pe_mix", (l, "dsp", c)))
                take((2,), (l, "o", c))
                for hd in range(4):
                    nc.tensor.matmul(bank4(2)[:, hd, 0:n], state[:, hd, :], qkv[:, hd, s0:s0 + n],
                                     start=True, stop=False)
                    last = nc.tensor.matmul(bank4(2)[:, hd, 0:n], lvl_x[:, 0, hd, :], qkg[:, b, hd, 0:n],
                                            start=False, stop=True)
                last.then_inc(*mark("pe_mix", (l, "op", c)))

            for grp in ((0, 1, 2), (3, 4)):
                for b, c in enumerate(grp):
                    chunk_setup(c, b)
                n = 0
                for lv in range(LEVELS):
                    for b, c in enumerate(grp):
                        level(c, b, lv, n + b)
                    for b, c in enumerate(grp):
                        level_y(c, b, lv, n + b)
                    if lv < LEVELS - 1:
                        for b, c in enumerate(grp):
                            level_t(c, b, lv, n + b)
                    n += len(grp)
                for b, c in enumerate(grp):
                    recur(c, b)
            for i in range(4):
                pe.wait_ge(*at((l, "o_sq", i)))
                take((4 + 2 * (i % 2), 5 + 2 * (i % 2)), (l, "o_rt", i))
                sum_rows(work2(i), tmp_s[:, i % 2, :], True, True).then_inc(*mark("pe_mix", (l, "o_ss", i)))
                tile_of(l, "c", i, 0, KD, h_hi, h_lo, PANEL0["c"] + i)
            pe.wait_ge(*at((l, "c_sq", 1)))
            take((4, 5), (l, "c_rt", 0))
            sum_rows(work2(0), kT[:, 2, :], True, False)
            sum_rows(work2(0), kT[:, 3, :], False, True).then_inc(*mark("pe_mix", (l, "c_ss", 0)))
            pe.wait_ge(*at((l, "c_sq", 2)))
            take((6, 7), (l, "c_rt", 1))
            sum_rows(work2(1), kT[:, 4, :], True, True).then_inc(*mark("pe_mix", (l, "c_ss", 1)))
            for m in range(KD):
                proj_tile(l, 0, m)
            pe.wait_ge(*at((l, "cn", 1)))
            for i in range(HEADS):
                tile_of(l, "uq", i, 2 * (i % 4), 2, cn_hi, cn_lo, PANEL0["uq"] + i // 4)
            pe.wait_ge(*at((l, "cn", 2)))
            for i in range(4):
                tile_of(l, "kn", i, i, 1, cn_hi[:, 2:3, :], cn_lo[:, 2:3, :], PANEL0["v"])
            s = (panel0(l) + PANEL0["v"]) % 2
            for c in range(NT):
                t = TILE0["v"] + c
                bt = (tile0(l) + t) % 2
                take((2 * bt, 2 * bt + 1), (l, "evac", t))
                w = slice(WIN[c], WIN[c] + P)
                mm3(psum[:, 2 * bt, :], cn_hi[:, 2, w], cn_lo[:, 2, w], w_hi[:, s, 512:1024], w_lo[:, s, 512:1024],
                    True, True).then_inc(*mark("tile_done", (l, "tile", t)))
            items = [(hd, i) for hd in range(HEADS) for i in range(NT)]

            def scores(n):
                hd, i = items[n]
                q0, qn = TILES[i]
                nk = q0 + qn
                b = 2 + 2 * (n % 3)
                if i == 0:
                    pe.wait_ge(*at((l, "evac", TILE0["uq"] + hd)))
                    pe.wait_ge(*at((l, "q_sum", hd)))
                    pe.wait_ge(*at((l, "evac", TILE0["kn"] + hd // 2)))
                    pe.wait_ge(*at((l, "kr", hd) if hd else (l, "k_rope")))
                take((b, b + 1), (l, "oT", n))
                for k0, k1 in ((0, min(256, nk)), (256, nk)):
                    if k1 > k0:
                        last = nc.tensor.matmul(flat(b, 256 + k0, k1 - k0)[0:qn], qT[0:QK, hd, q0:q0 + qn],
                                                kT[0:QK, hd, k0:k1], start=True, stop=True)
                last.then_inc(*mark("pe_mix", (l, "s", n)))

            def turn(n):
                hd, i = items[n]
                qn = TILES[i][1]
                pe.wait_ge(*at((l, "p", n)))
                take((0, 1), (l, "pT", n))
                for j in range(i + 1):
                    k0, kn = TILES[j]
                    last = nc.tensor.transpose(flat(0, P * j, qn)[0:kn], probs[0:qn, n % 2, k0:k0 + kn],
                                               ident[0:qn, 0:qn])
                last.then_inc(*mark("pe_mix", (l, "t", n)))

            def values(n):
                hd, i = items[n]
                qn = TILES[i][1]
                pe.wait_ge(*at((l, "pT", n)))
                b = 2 + 2 * (n % 3)
                r = VD * (hd % 2)
                for j in range(i + 1):
                    kn = TILES[j][1]
                    last = nc.tensor.matmul(psum[r:r + VD, b, 0:qn], v_tok[0:kn, j, hd * VD:(hd + 1) * VD],
                                            probsT[0:kn, n % 2, j, 0:qn], start=(j == 0), stop=(j == i))
                last.then_inc(*mark("pe_mix", (l, "pv", n)))

            pe.wait_ge(*at((l, "evac", TILE0["v"] + NT - 1)))
            scores(0)
            scores(1)
            for n in range(len(items)):
                if n:
                    values(n - 1)
                turn(n)
                if n + 2 < len(items):
                    scores(n + 2)
            values(len(items) - 1)

            for i in range(8):
                tile_of(l, "cv", i, 0, KD, h_hi, h_lo, PANEL0["cv"] + i)
            for m in range(KD):
                gates_tile(l, 1, m)
            for m in range(KD):
                gates_tile(l, 2, m)
                if m == 5:
                    take((4, 5), (l, "cv_mu"))
                    for i in range(4):
                        pe.wait_ge(*at((l, "cv_o", i)))
                        last = sum_rows(work2(0), cv_o[:, i, :], i == 0, i == 3)
                    last.then_inc(*mark("pe_mix", (l, "cv_sum")))
            take((6, 7), (l, "cv_rt"))
            for m in range(KD):
                proj_tile(l, 1, m)
                if m < 4:
                    pe.wait_ge(*at((l, "cv_sq", m)))
                    sum_rows(work2(1), tmp_s[:, m % 2, :], m == 0, m == 3).then_inc(*mark("pe_mix", (l, "cv_ss", m)))
            for m in range(KD):
                proj_tile(l, 2, m)

            pe.wait_ge(*at((l, "m", KD - 1)))
            take((4, 5), (l, "ln1", "mu"))
            for i in range(KD + 1):
                if i < KD:
                    tile_of(l, "mix", i, 0, KD, m_hi, m_lo, PANEL0["mix"] + i)
                if i:
                    pe.wait_ge(*at((l, "ln1", "x", i - 1)))
                    last = sum_rows(work2(0), acc[:, i - 1, :], i == 1, i == KD)
            last.then_inc(*mark("pe_ln", (l, "ln1", "sum")))

            def norm(which, wait):
                if wait:
                    take((4, 5), (l, which, "mu"))
                    for k in range(KD):
                        wait(k)
                        last = sum_rows(work2(0), acc[:, k, :], k == 0, k == KD - 1)
                    last.then_inc(*mark("pe_ln", (l, which, "sum")))
                take((6, 7), (l, which, "rt"))
                for k in range(KD):
                    pe.wait_ge(*at((l, which, "sq", k)))
                    sum_rows(work2(1), tmp_s[:, k % 2, :], k == 0, k == KD - 1)\
                        .then_inc(*mark("pe_ln", (l, which, "ss", k)))

            norm("ln1", None)

            if l == 1:
                take((4,), (l, "logits"))
                for c in range(NT):
                    for k in range(KD):
                        if c == 0:
                            pe.wait_ge(*at((l, "h_mid", k)))
                        last = mm3(psum[:, 4, 8 * c:8 * c + 8], h_hi[:, k, WIN[c]:WIN[c] + P],
                                   h_lo[:, k, WIN[c]:WIN[c] + P], router_hi[:, k, :], router_lo[:, k, :],
                                   k == 0, k == KD - 1)
                last.then_inc(*mark("rt_pe", (l, "rt_pe")))
            g0 = panel0(l) + MIX_PANELS
            t0 = tile0(l) + MIX_TILES
            if l == 0:
                take(range(8))
                for e in range(EXPERTS[0]):
                    def up(f, banks, j):
                        for part in range(2):
                            pe.wait_ge(lo_done[part], f + (e * (PER_EXPERT // 2) + g0 // 2 + 1))
                            if part == 0:
                                pe.wait_ge(silu_done, f + (e * F_TILES + 1))
                                pe.wait_ge(y_done, e * KD + 1)
                            else:
                                pe.wait_ge(act_done, f + (e * F_TILES + 1))
                            product(banks(part), ffn_w(l, j + part, 0), ffn_w(l, j + part, 1), 0, KD, h_hi, h_lo,
                                    (lambda k: pe.wait_ge(*at((l, "h_mid", k)))) if j + part == 0 else None)\
                                .then_inc(tile_done, 1)

                    j0 = e * PER_EXPERT
                    with nc.tensor.Fori(0, F_TILES // 2) as f2:
                        for y in range(2):
                            up(f2 * 2 + y, (pair, work2)[y], j0 + 2 * y)
                    up(F_TILES - 1, pair, j0 + 2 * (F_TILES - 1))
                    pe.wait_ge(actl_done, e * F_TILES + F_TILES)
                    with nc.tensor.Fori(0, KD // 4) as m4:
                        for y in range(4):
                            pe.wait_ge(lo_done[y % 2], m4 * 2 + ((g0 + j0) // 2 + F_TILES + y // 2 + 1))
                            pe.wait_ge(y_done, m4 * 4 + max(e * KD + y, 1))
                            j = j0 + 2 * F_TILES + y
                            product(pair(y), ffn_w(l, j, 0), ffn_w(l, j, 1), 0, F_TILES, act_hi, act_lo)\
                                .then_inc(tile_done, 1)
                counts.raised["tile_done"] += EXPERTS[l] * PER_EXPERT
                norm("ln2", lambda k: pe.wait_ge(y_done, 1 + EXPERTS[0] * KD - (KD - 1 - k)))
                continue

            def token_major(n):
                c, hf = n // 2, n % 2
                pe.wait_ge(*at((l, "full", 4 * hf + 3)))
                take((n % 4,), ("tok_lo", n))
                for j in range(4):
                    last = nc.tensor.transpose(bank4(n % 4)[:, j, :], acc[:, 4 * hf + j, WIN[c + 1]:WIN[c + 1] + P],
                                               ident[:])
                last.then_inc(*mark("rt_pe", ("tok", n)))

            for n in range(4):
                token_major(n)
            pe.wait_ge(*at("chosen"))
            take((5,), "slots", "load")
            for c in range(1, NT):
                dst = psum[:, 5, 8 * (c - 1):8 * c]
                for b in range(1, c):
                    nc.tensor.matmul(dst, ones[:], chosen[:, b, :], start=(b == 1), stop=False)
                nc.tensor.matmul(dst, cum_mask[:], chosen[:, c, :], start=(c == 1), stop=True)
            for c in range(1, NT):
                last = nc.tensor.matmul(psum[:, 5, 32:40], ones[:], chosen[:, c, :], start=(c == 1), stop=(c == NT - 1))
            last.then_inc(*mark("rt_pe", "columns"))
            for n in range(4, 8):
                token_major(n)

            take(range(8))

            def gather(slot, v1):
                pe.wait_ge(m_pick, v1 + 2)
                for m in range(KD):
                    b = 6 + m % 2
                    pe.wait_ge(m_x, v1 * KD + max(m - 1, 1) if m < 2 else v1 * KD + m)
                    for part, src in ((0, tok_hi), (1, tok_lo)):
                        for c in range(4):
                            last = nc.tensor.matmul(psum[:, b, part * CAP:(part + 1) * CAP],
                                                    src[:, c, m * P:(m + 1) * P], pick[:, slot, c, :],
                                                    start=(c == 0), stop=(c == 3))
                    last.then_inc(m_gather, 1)

            def scatter(v):
                pe.wait_ge(m_yhi, v * 4 + 1)
                pe.wait_ge(m_ylo, v * 4 + 1)
                for m in range(KD):
                    b = 4 + m % 2
                    pe.wait_ge(m_add, v * KD + max(m - 1, 1) if m < 2 else v * KD + m)
                    n = 0
                    for src in (yt_hi, yt_lo):
                        for c in range(2):
                            last = nc.tensor.matmul(psum[:, b, :], src[:, c, m * P:(m + 1) * P], put[:, c, :],
                                                    start=(n == 0), stop=(n == 3))
                            n += 1
                    last.then_inc(m_scat, 1)

            def products(b, j, nb, x):
                for k in range(nb):
                    cols = slice(k * P, (k + 1) * P)
                    nc.tensor.matmul(psum[:, b, 0:2 * CAP], ffn_w(l, j, 0)[:, cols],
                                     x[:, k].rearrange("p a n -> p (a n)"), start=(k == 0), stop=False)
                    last = nc.tensor.matmul(psum[:, b, 0:CAP], ffn_w(l, j, 1)[:, cols], x[:, k, 0, :],
                                            start=False, stop=(k == nb - 1))
                return last

            rounds = rounds_of(pe)
            gather(0, 0)
            with nc.tensor.Fori(0, rounds) as r:
                with nc.tensor.Fori(0, N_EXP // 2) as i:
                    for x in range(2):
                        v = r * N_EXP + i * 2 + x

                        def up(f, b, j):
                            for part in range(2):
                                pe.wait_ge(lo_done[part], v * (PER_EXPERT // 2) + f + (g0 // 2 + 1))
                                pe.wait_ge(m_x, v * KD + KD + 1)
                                if part == 0 and b == 0:
                                    pe.wait_ge(m_y, v * KD + 1)
                                elif part == 0:
                                    pe.wait_ge(m_ylo, v * 4 + 1)
                                    pe.wait_ge(m_yhi, v * 4 + 1)
                                pe.wait_ge(m_usum if part else m_gsum, v * F_TILES + f + 1)
                                products(2 * b + part, j + part, KD, xc).then_inc(tile_done, 1)

                        j0 = x * PER_EXPERT
                        with nc.tensor.Fori(0, F_TILES // 2) as f2:
                            for y in range(2):
                                up(f2 * 2 + y, y, j0 + 2 * y)
                        up(F_TILES - 1, 0, j0 + 2 * (F_TILES - 1))
                        scatter(v)
                        pe.wait_ge(m_put, v * 3 + 1)
                        pe.wait_ge(m_gsum, v * F_TILES + (F_TILES + 1))
                        pe.wait_ge(m_usum, v * F_TILES + (F_TILES + 1))
                        for ct in range(2):
                            cc = slice(ct * CT, (ct + 1) * CT)
                            for c in range(4):
                                last = nc.tensor.transpose(psum[0:CT, 2 + ct, c * P:(c + 1) * P],
                                                           pick[:, x, c, cc].bitcast(F32), ident[:])
                        last.then_inc(m_turn, 1)
                        pe.wait_ge(m_add, v * KD + KD)
                        for ct in range(2):
                            cc = slice(ct * CT, (ct + 1) * CT)
                            for c in range(4):
                                last = nc.tensor.matmul(psum[0:CT, 4, ct:ct + 1], pick[:, x, c, cc].bitcast(F32),
                                                        gates[:, c + 1, bass.ds(i * 2 + x, 1)],
                                                        start=(c == 0), stop=(c == 3))
                        last.then_inc(m_turn, 1)
                        gather(1 - x, v + 1)
                        for m in range(KD):
                            n = 2 * F_TILES + m
                            pe.wait_ge(lo_done[m % 2], v * (PER_EXPERT // 2) + ((g0 + n) // 2 + 1))
                            pe.wait_ge(ma_l, v * F_TILES + F_TILES + 1)
                            pe.wait_ge(m_y, v * KD + max(m - 1, 1) if m < 2 else v * KD + m)
                            products(m % 2, j0 + n, F_TILES, ma).then_inc(tile_done, 1)
                            if m:
                                turn_y(pe, v, m - 1)
                        turn_y(pe, v, KD - 1)
            scatter(rounds * N_EXP)
            norm("ln2", lambda k: pe.wait_ge(m_add, rounds * (N_EXP * KD) + (KD + 1)))

    @block.scalar
    def _(act):
        def fn(out_, in_, func, sem_, label, **kw):
            return nc.scalar.activation(out_, in_, func, **kw).then_inc(*mark(sem_, label))

        for s_ in (m_put, m_yhi, ma_h, m_silu):
            act.sem_inc(s_, 1)
        act.sem_inc(silu_done, 2)
        def heads_mix(l, p):
            g = panel0(l) + p
            act.wait_ge(raw_in[g % RAW], 16 * (g // RAW + 1))
            if p >= 2:
                act.wait_ge(*at((l, "tile", LAST_TILE[p - 2])))
            elif l > 0:
                act.wait_ge(tile_done, tile0(l) - 1 + p)
            nc.scalar.activation(w_hi[:, g % 2, 0:WIDE], raw[:, g % RAW, 0:WIDE], ACT.Copy).then_inc(hi_done, 1)

        def after(l, name, i):
            t = TILE0[name] + i
            for p in range(2, MIX_PANELS):
                if LAST_TILE[p - 2] == t:
                    heads_mix(l, p)

        act.wait_ge(*at("eps"))
        heads_mix(0, 0)
        heads_mix(0, 1)
        for l in range(DEPTH):
            if l == 0:
                for k in range(KD):
                    act.wait_ge(h_in[k // 2], 16)
                    fn(h_hi[:, k, :], acc[:, k, :], ACT.Copy, "act_ln", ("h0_hi", k))
            act.wait_ge(vec_in, 16 * (l + 1))
            for i in range(12 + 2):
                if i < 12:
                    t = TILE0["qkv"] + i
                    act.wait_ge(*at((l, "tile", t)))
                    if i >= 2:
                        act.wait_ge(*at((l, "conv", i - 2)))
                    fn(halves(x_pad[:, i % 2, 3:3 + T]), pair(tile0(l) + t), ACT.Copy, "act_mix", (l, "evac", t))
                    after(l, "qkv", i)
                if i >= 1 and i - 1 < 12:
                    j = i - 1
                    act.wait_ge(*at((l, "conv", j)))
                    fn(qkv[:, j, :], conv_o[:, j % 2, :], ACT.Silu, "act_mix", (l, "qkv", j))
            t = TILE0["ba"]
            act.wait_ge(*at((l, "tile", t)))
            fn(ba[:].rearrange("p a b -> p (a b)"), psum[:, 2 * ((tile0(l) + t) % 2), 0:8 * NT], ACT.Copy,
               "act_mix", (l, "evac", t))
            after(l, "ba", 0)
            act.wait_ge(*at((l, "qkv", 11)))

            def qk_square(i):
                if i >= 2:
                    act.wait_ge(*at((l, "qk_ss", i - 2)))
                fn(tmp_s[:, i % 2, :], qkv[:, i, :], ACT.Square, "act_mix", (l, "qk_sq", i))

            def gate_tile(n, m):
                t = TILE0[f"g{n}"] + m
                act.wait_ge(*at((l, "tile", t)))
                fn(halves(gate_of(n, m)), pair(tile0(l) + t), ACT.Sigmoid, "act_mix", (l, "evac", t))
                after(l, f"g{n}", m)

            qk_square(0)
            qk_square(1)
            for j in range(8):
                act.wait_ge(*at((l, "qk_ss", j)))
                if j >= 2:
                    act.wait_ge(*at((l, "qkn", j - 2)))
                fn(halves(gate_s[:, j % 2, :]), work2(j), ACT.Sqrt, "act_mix", (l, "qk_rt", j), bias=eps[:, 0:1])
                if j + 2 < 8:
                    qk_square(j + 2)
                gate_tile(0, j)
            fn(b_tok[:], ba[:, :, 0:4], ACT.Sigmoid, "act_mix", (l, "beta"))
            act.wait_ge(*at((l, "a_dt")))
            fn(sp2[:], sp1[:], ACT.Abs, "act_mix", (l, "a_abs"))
            act.wait_ge(*at((l, "a_abs")))
            fn(sp2[:], sp2[:], ACT.Exp, "act_mix", (l, "a_exp"), scale=-1.0)
            fn(ea[:], vec[:, VEC["a_log"]:VEC["a_log"] + 4], ACT.Exp, "act_mix", (l, "ea"))
            act.wait_ge(*at((l, "a_exp")))
            fn(sp2[:], sp2[:], ACT.Ln, "act_mix", (l, "a_ln"), bias=1.0)

            def chunk_setup(c, b):
                act.wait_ge(*at((l, "cum", c)))
                fn(cums[:, c, :], psum[:, 4, 0:8], ACT.Copy, "act_mix", (l, "cum_s", c))
                act.wait_ge(*at((l, "cum_s", c)))
                fn(ecum[:, c, :], cums[:, c, :], ACT.Exp, "act_mix", (l, "ecum", c))
                act.wait_ge(*at((l, "tot", c)))
                fn(eneg[:, c, :], eneg[:, c, :], ACT.Exp, "act_mix", (l, "eneg", c))
                act.wait_ge(*at((l, "diff", c)))
                fn(lvl_x[:, 0], bank4(5), ACT.Exp, "act_mix", (l, "eB", c))
                act.wait_ge(*at((l, "diffm", c)))
                fn(wk[:, 1], wk[:, 1], ACT.Exp, "act_mix", (l, "gam", c))
                act.wait_ge(*at((l, "vtr", c)))
                fn(vtok[:, b], bank4(1), ACT.Copy, "act_mix", (l, "vtok", c))
                if c < 4:
                    t = TILE0["z"] + c
                    act.wait_ge(*at((l, "tile", t)))
                    fn(halves(z_s[:, c, :]), work2(1), ACT.Silu, "act_mix", (l, "evac", t))
                    after(l, "z", c)

            def level(c, b, lv, n):
                act.wait_ge(*at((l, "Xp", c, lv)))
                fn(lvl_x[:, n % 3], bank4(n % 3), ACT.Copy, "act_mix", (l, "X", c, lv))

            def level_t(c, b, lv, n):
                act.wait_ge(*at((l, "Tp", c, lv)))
                fn(dN[:, b], bank4(n % 3), ACT.Copy, "act_mix", (l, "dN", c, lv))

            def recur(c, b):
                s0, n = TILES[c]
                act.wait_ge(*at((l, "up", c)))
                fn(lvl_x[:, 0], bank4(1), ACT.Copy, "act_mix", (l, "u", c))
                act.wait_ge(*at((l, "op", c)))
                fn(qkv[:, 0:4, s0:s0 + n], bank4(2)[:, :, 0:n], ACT.Copy, "act_mix", (l, "o", c))

            for grp in ((0, 1, 2), (3, 4)):
                for b, c in enumerate(grp):
                    chunk_setup(c, b)
                n = 0
                for lv in range(LEVELS):
                    for b, c in enumerate(grp):
                        level(c, b, lv, n + b)
                    if lv < LEVELS - 1:
                        for b, c in enumerate(grp):
                            level_t(c, b, lv, n + b)
                    n += len(grp)
                for b, c in enumerate(grp):
                    recur(c, b)
            act.wait_ge(*at((l, "o", NT - 1)))

            def o_square(i):
                if i >= 2:
                    act.wait_ge(*at((l, "o_ss", i - 2)))
                fn(tmp_s[:, i % 2, :], qkv[:, i, :], ACT.Square, "act_mix", (l, "o_sq", i))

            o_square(0)
            o_square(1)
            for i in range(4):
                act.wait_ge(*at((l, "o_ss", i)))
                fn(halves(qkv[:, 4 + i, :]), work2(i), ACT.Sqrt, "act_mix", (l, "o_rt", i),
                   bias=eps[:, 0:1], scale=1.0 / P)
                if i < 2:
                    o_square(i + 2)
                if i < 3:
                    t = TILE0["c"] + i
                    act.wait_ge(*at((l, "tile", t)))
                    fn(halves(c_f[:, i, :]), pair(tile0(l) + t), ACT.Copy, "act_mix", (l, "evac", t))
                    after(l, "c", i)
                    act.wait_ge(*at((l, "evac", t)))
                    fn(kT[:, 2 + i, :], c_f[:, i, :], ACT.Square, "act_mix", (l, "c_sq", i))
            after(l, "c", 3)

            def split_hi(n):
                for i in range(4):
                    act.wait_ge(*at((l, "br_f", n, i) if n != 1 else (l, "oT", HEADS * NT - 1)))
                    fn(br_hi[:, i, :], branch_src(n)[:, i, :], ACT.Copy, "act_mix", (l, "br_hi", n, i))

            split_hi(0)

            act.wait_ge(*at((l, "br", 0)))
            act.wait_ge(*at((l, "c_ss", 0)))
            fn(halves(qT[:, 0, :]), work2(0), ACT.Sqrt, "act_mix", (l, "c_rt", 0), bias=eps[:, 0:1], scale=1 / 256)
            act.wait_ge(*at((l, "c_ss", 1)))
            fn(halves(qT[:, 1, :]), work2(1), ACT.Sqrt, "act_mix", (l, "c_rt", 1), bias=eps[:, 0:1], scale=1 / 128)
            after(l, "p0", 1)
            after(l, "p0", 3)
            for i in range(3):
                act.wait_ge(*at((l, "cf", i)))
                fn(cn_hi[:, i, :], c_f[:, i, :], ACT.Copy, "act_mix", (l, "cn_hi", i))
            after(l, "p0", 5)
            after(l, "p0", 7)
            act.wait_ge(*at((l, "k_rope")))
            for hd in range(1, HEADS):
                fn(kT[NOPE:QK, hd, :], kT[NOPE:QK, 0, :], ACT.Copy, "act_mix", (l, "kr", hd))
            for hd in range(HEADS):
                t = TILE0["uq"] + hd
                act.wait_ge(*at((l, "tile", t)))
                act.wait_ge(*at((l, "q_rope", hd)))
                if hd < 2:
                    act.wait_ge(*at((l, "cf", 2)))
                fn(halves(qT[0:NOPE, hd, :]), pair(tile0(l) + t)[0:NOPE], ACT.Copy, "act_mix", (l, "evac", t))
                after(l, "uq", hd)
            for i in range(4):
                t = TILE0["kn"] + i
                act.wait_ge(*at((l, "tile", t)))
                fn(halves(kT[0:NOPE, 2 * i, :]), pair(tile0(l) + t)[0:NOPE], ACT.Copy, "act_mix", (l, "kn0", i))
                fn(halves(kT[0:NOPE, 2 * i + 1, :]), pair(tile0(l) + t)[NOPE:P], ACT.Copy, "act_mix", (l, "evac", t))
            for c in range(NT):
                t = TILE0["v"] + c
                act.wait_ge(*at((l, "tile", t)))
                fn(v_tok[:, c, :], psum[:, 2 * ((tile0(l) + t) % 2), :], ACT.Copy, "act_mix", (l, "evac", t))
                after(l, "v", c)
            items = [(hd, i) for hd in range(HEADS) for i in range(NT)]

            def pt_evac(n):
                hd, i = items[n]
                qn = TILES[i][1]
                act.wait_ge(*at((l, "t", n)))
                if n >= 2:
                    act.wait_ge(*at((l, "pv", n - 2)))
                fn(probsT[0:N_META, n % 2, 0, 0:qn], flat(0, 0, qn)[0:N_META], ACT.Copy, "act_mix",
                   (l, "pT0", n) if i else (l, "pT", n))
                if i:
                    fn(probsT[:, n % 2, 1:i + 1, :], flat(0, P, P * i).rearrange("p (j n) -> p j n", n=P), ACT.Copy,
                       "act_mix", (l, "pT", n))

            def o_evac(n):
                hd, i = items[n]
                q0, qn = TILES[i]
                r = VD * (hd % 2)
                act.wait_ge(*at((l, "pv", n)))
                fn(att_o[r:r + VD, hd // 2, q0:q0 + qn], psum[r:r + VD, 2 + 2 * (n % 3), 0:qn], ACT.Copy, "act_mix",
                   (l, "oT", n))

            def exps(n):
                hd, i = items[n]
                q0, qn = TILES[i]
                nk = q0 + qn
                act.wait_ge(*at((l, "nmax", n)))
                if n >= 2:
                    act.wait_ge(*at((l, "t", n - 2)))
                fn(probs[0:qn, n % 2, 0:nk], flat(2 + 2 * (n % 3), 256, nk)[0:qn], ACT.Exp, "act_mix",
                   (l, "exp", n), bias=stat[0:qn, n % 3, 1:2], scale=QK ** -0.5,
                   accum_out=stat[0:qn, n % 3, 2:3])

            exps(0)
            for n in range(len(items) + 1):
                if n + 1 < len(items):
                    exps(n + 1)
                if n:
                    o_evac(n - 1)
                if n < len(items):
                    pt_evac(n)
            split_hi(1)

            act.wait_ge(*at((l, "br", 1)))
            for i in range(4):
                for part, dst in ((0, u_pad[:, i, CV_W - 1:]), (1, cv_o[:, i, :])):
                    t = TILE0["cv"] + 2 * i + part
                    act.wait_ge(*at((l, "tile", t)))
                    fn(halves(dst), pair(tile0(l) + t), ACT.Sigmoid if part else ACT.Copy, "act_mix", (l, "evac", t))
                    after(l, "cv", 2 * i + part)
            for m in range(KD):
                gate_tile(1, m)
            for m in range(KD):
                gate_tile(2, m)
                if m == 5:
                    act.wait_ge(*at((l, "cv_sum")))
                    fn(halves(gate_s[:, 0, :]), work2(0), ACT.Copy, "act_mix", (l, "cv_mu"), scale=1 / 512)
            for i in range(4):
                act.wait_ge(*at((l, "cv_c", i)))
                if i >= 2:
                    act.wait_ge(*at((l, "cv_ss", i - 2)))
                fn(tmp_s[:, i % 2, :], cv_o[:, i, :], ACT.Square, "act_mix", (l, "cv_sq", i))
                after(l, "p1", i)
            act.wait_ge(*at((l, "cv_ss", 3)))
            fn(halves(gate_s[:, 1, :]), work2(1), ACT.Sqrt, "act_mix", (l, "cv_rt"), bias=eps[:, 0:1], scale=1 / 512)
            after(l, "p1", 5)
            for i in range(4):
                act.wait_ge(*at((l, "cv_n", i)))
                fn(cv_o[:, i, :], cv_o[:, i, :], ACT.Silu, "act_mix", (l, "br_f", 2, i), bias=vcol("cvlb", i))
            after(l, "p1", 7)
            split_hi(2)
            for m in range(KD):
                act.wait_ge(*at((l, "merged", m)))
                fn(m_hi[:, m, :], acc[:, m, :], ACT.Copy, "act_mix", (l, "m_hi", m))
                after(l, "p2", m)
            for m in range(KD):
                after(l, "mix", m)

            t0 = (l + 1) * MIX_TILES + EXP0[l] * PER_EXPERT
            g0 = (l + 1) * MIX_PANELS + EXP0[l] * PER_EXPERT
            def token_major(n):
                act.wait_ge(*at(("tok", n)))
                fn(tok_hi[:, n // 2, 512 * (n % 2):512 * (n % 2) + 512], psum[:, n % 4, :], ACT.Copy, "rt_act",
                   ("tok_hi", n))

            act.wait_ge(lo_done[0], g0 // 2)
            act.wait_ge(lo_done[1], g0 // 2)

            def heads(n, before):
                cols = WIDE if n % PER_EXPERT < 2 * F_TILES else DEEP
                act.wait_ge(raw_in[n % RAW], before * (16 // RAW) + 16 * ((g0 + n) // RAW + 1))
                act.wait_ge(tile_done, before + (t0 + n - 3))
                nc.scalar.activation(ffn_w(l, n, 0)[:, 0:cols], raw[:, n % RAW, 0:cols], ACT.Copy).then_inc(hi_done, 1)

            def norm(which):
                act.wait_ge(*at((l, which, "sum")))
                fn(halves(gate_s[:, 0, :]), work2(0), ACT.Copy, "act_ln", (l, which, "mu"), scale=1 / D)
                for k in range(KD):
                    act.wait_ge(*at((l, which, "c", k)))
                    if k >= 2:
                        act.wait_ge(*at((l, which, "ss", k - 2)))
                    fn(tmp_s[:, k % 2, :], acc[:, k, :], ACT.Square, "act_ln", (l, which, "sq", k))
                act.wait_ge(*at((l, which, "ss", KD - 1)))
                fn(halves(gate_s[:, 1, :]), work2(1), ACT.Sqrt, "act_ln", (l, which, "rt"), bias=eps[:, 0:1],
                   scale=1 / D)
                if which == "ln1":
                    for n in range(2):
                        heads(n, 0)
                last = which == "ln2" and l == DEPTH - 1
                for k in range(KD):
                    act.wait_ge(*at((l, which, "n", k)))
                    fn(acc[:, k, :] if last else h_hi[:, k, :], acc[:, k, :], ACT.Identity, "act_ln",
                       (l, which, "out" if last else "hi", k), bias=vcol(which + "b", k))
                if which == "ln1" and l == 1:
                    for k in range(KD):
                        act.wait_ge(*at((l, "h_mid", k)))
                        fn(acc[:, k, :], acc[:, k, :], ACT.Identity, "act_ln", (l, "full", k), bias=vcol("ln1b", k))

            norm("ln1")

            if l == 0:
                for n in range(2, AHEAD):
                    heads(n, 0)
                for e in range(EXPERTS[0]):
                    for f in range(F_TILES):
                        n = e * PER_EXPERT + 2 * f
                        cnt = e * F_TILES + f
                        act.wait_ge(tile_done, t0 + n + 1)
                        act.wait_ge(act_done, cnt + 1)
                        nc.scalar.activation(halves(gate_s[:, f % 2, :]), (pair, work2)[f % 2](0), ACT.Silu).then_inc(silu_done, 1)
                        heads(n + 4, 0)
                        act.wait_ge(act_done, cnt + 3)
                        nc.scalar.activation(act_hi[:, f, :], act_f[:, f % 2, :], ACT.Copy).then_inc(acth_done, 1)
                        heads(n + 5, 0)
                    for m in range(KD):
                        n = e * PER_EXPERT + 2 * F_TILES + m
                        if n + AHEAD < 2 * PER_EXPERT:
                            heads(n + AHEAD, 0)
                act.wait_ge(lo_done[0], panel0(l + 1) // 2)
                act.wait_ge(lo_done[1], panel0(l + 1) // 2)
                heads_mix(l + 1, 0)
                heads_mix(l + 1, 1)
                norm("ln2")
                act.wait_ge(*at((l + 1, "h", KD - 1)))
                act.dma_start(vec[:], ins["vec"][l + 1]).then_inc(vec_in, 16)
                continue

            act.wait_ge(*at((l, "rt_pe")))
            act.dma_start(column_no[:], ins["column_no"]).then_inc(const_in, 16)
            fn(logits[:].rearrange("p a b -> p (a b)"), psum[:, 4, 0:8 * NT], ACT.Copy, "rt_act", (l, "logits"))
            for n in range(4):
                token_major(n)
            act.wait_ge(*at((l, "w_arg")))
            fn(top_w[:, :, 1:2], top_w[:, :, 1:2], ACT.Exp, "rt_act", (l, "w_exp"))
            for n in range(2, AHEAD):
                heads(n, 0)
            for n in range(4, 8):
                token_major(n)
            for m in range(KD):
                fn(acc[:, m, :], acc[:, m, :], ACT.Copy, "rt_act", ("scaled", m), scale=ALPHA)
            rounds = rounds_of(act)
            with nc.scalar.Fori(0, rounds) as r:
                with nc.scalar.Fori(0, N_EXP // 2) as i:
                    before = r * (N_EXP * PER_EXPERT) + i * (2 * PER_EXPERT)
                    for x in range(2):
                        v = r * N_EXP + i * 2 + x
                        for f in range(F_TILES):
                            n = x * PER_EXPERT + 2 * f
                            act.wait_ge(m_gsum, v * F_TILES + (f + 3))
                            nc.scalar.activation(moe_g[:, f % 2, :], moe_g[:, f % 2, :], ACT.Silu).then_inc(m_silu, 1)
                            heads(n + 4, before)
                            act.wait_ge(m_act, v * F_TILES + (f + 3))
                            nc.scalar.activation(ma[:, f, 0, :], moe_a[:, f % 2, :], ACT.Copy).then_inc(ma_h, 1)
                            heads(n + 5, before)
                        act.wait_ge(m_turn, v * 2 + 2)
                        for ct in range(2):
                            nc.scalar.activation(put[:, ct, :], psum[0:CT, 2 + ct, :], ACT.Copy).then_inc(m_put, 1)
                        act.wait_ge(m_turn, v * 2 + 3)
                        nc.scalar.activation(gate_c[:], psum[0:CT, 4, 0:2], ACT.Copy).then_inc(m_put, 1)
                        for m in range(KD):
                            n = x * PER_EXPERT + 2 * F_TILES + m
                            heads(n + AHEAD, before)
                            if m % 4 == 3:
                                act.wait_ge(m_yt, v * KD + m + 2)
                                act.wait_ge(m_put, v * 3 + 4)
                                half = slice(512 * (m // 4), 512 * (m // 4) + 512)
                                for ct in range(2):
                                    nc.scalar.activation(yt_hi[:, ct, half], psum[0:CT, 2 + ct, :], ACT.Copy,
                                                         scale=gate_c[:, ct:ct + 1]).then_inc(m_yhi, 1)
            norm("ln2")

    @block.vector
    def _(dve):
        def tt(out_, a, b, op, sem_, label):
            return nc.vector.tensor_tensor(out_, a, b, op).then_inc(*mark(sem_, label))

        def ts(out_, a, s1, s2, op0, op1, sem_, label):
            if s2 is None:
                return nc.vector.tensor_scalar(out_, a, s1, None, op0).then_inc(*mark(sem_, label))
            return nc.vector.tensor_scalar(out_, a, s1, s2, op0, op1).then_inc(*mark(sem_, label))

        def stt(out_, a, s, b, op0, op1, sem_, label):
            return nc.vector.scalar_tensor_tensor(out=out_, in0=a, scalar=s, in1=b, op0=op0, op1=op1)\
                .then_inc(*mark(sem_, label))

        def remainder(lo, full, hi, sem_, label):
            return tt(lo, full, hi.bitcast(F32), ALU.subtract, sem_, label)

        for s_ in (y_done, m_pick, m_x, m_y, ma_l, m_ylo, m_add):
            dve.sem_inc(s_, 1)
        for s_ in (act_done, m_gsum, m_usum, m_act):
            dve.sem_inc(s_, 2)
        for l in range(DEPTH):
            if l == 0:
                for k in range(KD):
                    dve.wait_ge(*at(("h0_hi", k)))
                    remainder(h_lo[:, k, :], acc[:, k, :], h_hi[:, k, :], "dve_ln",
                              (0, "h", k))
                dve.wait_ge(const_in, 144)
                nc.vector.tensor_copy(router_hi[:], router[:]).then_inc(*mark("rt_dve", "router_hi"))
                dve.wait_ge(*at("router_hi"))
                remainder(router_lo[:], router[:], router_hi[:], "rt_dve", "router_lo")
            dve.wait_ge(vec_in, 16 * (l + 1))
            nc.vector.memset(x_pad[:, :, 0:3], 0.0).then_inc(*mark("dve_mix", (l, "pad")))
            dve.wait_ge(*at((l, "pad")))
            for i in range(12):
                t = TILE0["qkv"] + i
                dve.wait_ge(*at((l, "evac", t)))
                if i >= 2:
                    dve.wait_ge(*at((l, "qkv", i - 2)))
                for w in range(4):
                    src = x_pad[:, i % 2, w:w + T]
                    label = (l, "conv", i) if w == 3 else (l, "conv", i, w)
                    if w == 0:
                        ts(conv_o[:, i % 2, :], src, vcol("conv", 4 * i), None, ALU.mult, None, "dve_mix", label)
                    else:
                        dve.wait_ge(*at((l, "conv", i, w - 1)))
                        stt(conv_o[:, i % 2, :], src, vcol("conv", 4 * i + w), conv_o[:, i % 2, :], ALU.mult, ALU.add,
                            "dve_mix", label)
            for i in range(8):
                dve.wait_ge(*at((l, "qk_rt", i)))
                nc.vector.reciprocal(gate_s[:, i % 2, :], gate_s[:, i % 2, :]).then_inc(*mark("dve_mix", (l, "qk_r", i)))
                dve.wait_ge(*at((l, "qk_r", i)))
                dve.wait_ge(*at((l, "qkv", i)))
                stt(qkv[:, i, :], qkv[:, i, :], P ** -0.5 if i < 4 else 1.0, gate_s[:, i % 2, :], ALU.mult, ALU.mult,
                    "dve_mix", (l, "qkn", i))
            dve.wait_ge(*at((l, "evac", TILE0["ba"])))
            tt(sp1[:], ba[:, :, 4:8], bc(vec[:, VEC["dt"]:VEC["dt"] + 4], 1, NT), ALU.add, "dve_mix", (l, "a_dt"))
            dve.wait_ge(*at((l, "a_ln")))
            stt(sp1[:], sp1[:], 0.0, sp2[:], ALU.max, ALU.add, "dve_mix", (l, "sp"))
            dve.wait_ge(*at((l, "sp")))
            stt(sp1[:], sp1[:], -1.0, bc(ea[:], 1, NT), ALU.mult, ALU.mult, "dve_mix", (l, "g_all"))
            dve.wait_ge(*at((l, "g_all")))
            tt(g_tok[:], sp1[:], meta_rows[:], ALU.mult, "dve_mix", (l, "g"))
            tt(b_tok[:], b_tok[:], meta_rows[:], ALU.mult, "dve_mix", (l, "beta_m"))
            dve.wait_ge(*at((l, "qkn", 7)))
            nc.vector.memset(state[:], 0.0).then_inc(*mark("dve_mix", (l, "state0")))
            dve.wait_ge(*at((l, "state0")))

            def chunk_setup(c, b):
                s0, n = TILES[c]
                if c:
                    dve.wait_ge(*at((l, "cumB", c - 1)))
                nc.vector.tensor_copy(wk[:, 0], bc(g_tok[:, c, :], 2, P)).then_inc(*mark("dve_mix", (l, "gb", c)))
                dve.wait_ge(*at((l, "cum_s", c)))
                tt(eneg[:, c, :], cums[:, c, 4:8], cums[:, c, 0:4], ALU.subtract, "dve_mix", (l, "tot", c))
                dve.wait_ge(*at((l, "cumB", c)))
                if c:
                    dve.wait_ge(*at((l, "aT", c - 1)))
                tt(wk[:, 1], bank4(5), bc(cums[:, c, 0:4], 2, P), ALU.subtract, "dve_mix", (l, "diff", c))
                dve.wait_ge(*at((l, "diff", c)))
                tt(wk[:, 1], wk[:, 1], bc(neg_ji[:], 1, 4), ALU.add, "dve_mix", (l, "diffm", c))
                dve.wait_ge(*at((l, "gam", c)))
                dve.wait_ge(*at((l, "qk", c)))
                tt(qkg[:, b], bank4(4), wk[:, 1], ALU.mult, "dve_mix", (l, "qkg", c))
                dve.wait_ge(*at((l, "qkg", c)))
                dve.wait_ge(*at((l, "kk", c)))
                tt(wk[:, 1], bank4(3), wk[:, 1], ALU.mult, "dve_mix", (l, "m1", c))
                dve.wait_ge(*at((l, "eB", c)))
                tt(qkv[:, 0:4, s0:s0 + n], qkv[:, 0:4, s0:s0 + n], lvl_x[:, 0, :, 0:n], ALU.mult, "dve_mix",
                   (l, "qdec", c))
                dve.wait_ge(*at((l, "eneg", c)))
                dve.wait_ge(*at((l, "ktok", c)))
                tt(kdec[:, b], bank4(0), bc(eneg[:, c, :], 2, P), ALU.mult, "dve_mix", (l, "kdec", c))
                dve.wait_ge(*at((l, "aT", c)))
                tt(aN[:, b], bank4(2), bc(b_tok[:, c, :], 2, P), ALU.mult, "dve_mix", (l, "aN", c))
                dve.wait_ge(*at((l, "aN", c)))
                dve.wait_ge(*at((l, "qdec", c)))

            def level_e(c, b, lv, n):
                tt(lvl_e[:, n % 3], aN[:, b], bc(level_mask[:, lv, :], 1, 4), ALU.mult, "dve_mix", (l, "E", c, lv))

            def level(c, b, lv, n):
                dve.wait_ge(*at((l, "Yp", c, lv)))
                base = dT[:, b] if lv else bc(ident[:], 1, 4)
                if lv:
                    dve.wait_ge(*at((l, "dT", c, lv - 1)))
                tt(dT[:, b], base, bank4(3 + n % 3), ALU.subtract, "dve_mix", (l, "dT", c, lv))

            def recur(c, b):
                dve.wait_ge(*at((l, "dT", c, LEVELS - 1)))
                tt(dT[:, b], dT[:, b], bc(b_tok[:, c, :], 2, P), ALU.mult, "dve_mix", (l, "TT", c))
                dve.wait_ge(*at((l, "ks", c)))
                dve.wait_ge(*at((l, "ecum", c)))
                tt(lvl_e[:, 0], bank4(0), bc(ecum[:, c, 0:4], 2, P), ALU.mult, "dve_mix", (l, "r1", c))
                dve.wait_ge(*at((l, "r1", c)))
                dve.wait_ge(*at((l, "vtok", c)))
                tt(lvl_e[:, 0], vtok[:, b], lvl_e[:, 0], ALU.subtract, "dve_mix", (l, "R", c))
                dve.wait_ge(*at((l, "op", c)))
                if c:
                    dve.wait_ge(*at((l, "ds", c - 1)))
                tt(state[:], state[:], bc(ecum[:, c, 4:8], 2, P), ALU.mult, "dve_mix", (l, "sd", c))
                dve.wait_ge(*at((l, "dsp", c)))
                dve.wait_ge(*at((l, "sd", c)))
                tt(state[:], state[:], bank4(3), ALU.add, "dve_mix", (l, "ds", c))

            for grp in ((0, 1, 2), (3, 4)):
                for b, c in enumerate(grp):
                    chunk_setup(c, b)
                seq = [(lv, b, c, lv * len(grp) + b) for lv in range(LEVELS) for b, c in enumerate(grp)]
                ahead = len(grp)
                for x in range(len(seq) + ahead):
                    if x < len(seq):
                        lv, b, c, n = seq[x]
                        if x >= 3:
                            dve.wait_ge(*at((l, "Xp", seq[x - 3][2], seq[x - 3][0])))
                        level_e(c, b, lv, n)
                    if x >= ahead:
                        lv, b, c, n = seq[x - ahead]
                        level(c, b, lv, n)
                for b, c in enumerate(grp):
                    recur(c, b)
            for i in range(4):
                dve.wait_ge(*at((l, "o_rt", i)))
                nc.vector.reciprocal(qkv[:, 4 + i, :], qkv[:, 4 + i, :]).then_inc(*mark("dve_mix", (l, "o_r", i)))
                dve.wait_ge(*at((l, "o_r", i)))
                stt(qkv[:, i, :], qkv[:, i, :], vcol("o_norm"), qkv[:, 4 + i, :], ALU.mult, ALU.mult, "dve_mix",
                    (l, "o_n", i))
            for i in range(4):
                dve.wait_ge(*at((l, "evac", TILE0["z"] + i)))
                dve.wait_ge(*at((l, "o_n", i)))
                tt(qkv[:, i, :], qkv[:, i, :], z_s[:, i, :], ALU.mult, "dve_mix", (l, "br_f", 0, i))

            def split_lo(n):
                for i in range(4):
                    dve.wait_ge(*at((l, "br_hi", n, i)))
                    remainder(br_lo[:, i, :], branch_src(n)[:, i, :], br_hi[:, i, :], "dve_mix",
                              (l, "br", n) if i == 3 else (l, "br_lo", n, i))

            def merge(n, m):
                t = TILE0[f"p{n}"] + m
                dve.wait_ge(*at((l, "evac", TILE0[f"g{n}"] + m)))
                dve.wait_ge(*at((l, "tile", t)))
                if n == 0:
                    tt(halves(acc[:, m, :]), pair(tile0(l) + t), halves(acc[:, m, :]), ALU.mult, "dve_mix",
                       (l, "evac", t))
                    return
                g = gate_of(n, m)
                tt(halves(g), pair(tile0(l) + t), halves(g), ALU.mult, "dve_mix", (l, "evac", t))
                dve.wait_ge(*at((l, "evac", t)))
                dve.wait_ge(*at(gy(l, 0, m) if n == 1 else (l, "merge", 1, m)))
                tt(acc[:, m, :], acc[:, m, :], g, ALU.add, "dve_mix", (l, "merge", n, m) if n == 1 else (l, "merged", m))

            split_lo(0)

            t = TILE0["c"] + 3
            dve.wait_ge(*at((l, "tile", t)))
            dve.wait_ge(*at((l, "br", 0)))
            kr = pair(tile0(l) + t)
            r0, r1 = slice(NOPE, QK), slice(QK, P)
            tt(halves(kT[r0, 0, :]), kr[r0], halves(rope[r0, :]), ALU.mult, "dve_mix", (l, "kr_c"))
            tt(halves(kT[r0, 1, :]), kr[r1], halves(rope[r1, :]), ALU.mult, "dve_mix", (l, "evac", t))
            dve.wait_ge(*at((l, "kr_c")))
            dve.wait_ge(*at((l, "evac", t)))
            tt(kT[r0, 0, :], kT[r0, 0, :], kT[r0, 1, :], ALU.add, "dve_mix", (l, "k_rope"))
            merge(0, 0)
            merge(0, 1)
            for i in range(3):
                r = qT[:, i // 2, :]
                if i != 1:
                    dve.wait_ge(*at((l, "c_rt", i // 2)))
                    nc.vector.reciprocal(r, r).then_inc(*mark("dve_mix", (l, "c_r", i // 2)))
                    dve.wait_ge(*at((l, "c_r", i // 2)))
                stt(c_f[:, i, :], c_f[:, i, :], vcol("q_norm", i) if i < 2 else vcol("kv_norm"), r, ALU.mult, ALU.mult,
                    "dve_mix", (l, "cf", i))
                merge(0, 2 + i)
            for i in range(3):
                dve.wait_ge(*at((l, "cn_hi", i)))
                remainder(cn_lo[:, i, :], c_f[:, i, :], cn_hi[:, i, :], "dve_mix", (l, "cn", i))
                merge(0, 5 + i)
            for hd in range(HEADS):
                t = TILE0["uq"] + hd
                dve.wait_ge(*at((l, "tile", t)))
                if hd < 2:
                    dve.wait_ge(*at((l, "cf", 2)))
                if hd >= 1:
                    dve.wait_ge(*at((l, "q_sum", hd - 1)))
                qr = pair(tile0(l) + t)
                tt(halves(qT[r0, hd, :]), qr[r0], halves(rope[r0, :]), ALU.mult, "dve_mix", (l, "q_c", hd))
                tt(halves(c_f[r0, 0, :]), qr[r1], halves(rope[r1, :]), ALU.mult, "dve_mix", (l, "q_rope", hd))
                dve.wait_ge(*at((l, "q_rope", hd)))
                tt(qT[r0, hd, :], qT[r0, hd, :], c_f[r0, 0, :], ALU.add, "dve_mix", (l, "q_sum", hd))
            items = [(hd, i) for hd in range(HEADS) for i in range(NT)]
            SC = QK ** -0.5

            def normalise(n):
                hd, i = items[n]
                q0, qn = TILES[i]
                nk = q0 + qn
                dve.wait_ge(*at((l, "exp", n)))
                st = stat[0:qn, n % 3]
                nc.vector.reciprocal(st[:, 3:4], st[:, 2:3]).then_inc(*mark("dve_mix", (l, "rinv", n)))
                dve.wait_ge(*at((l, "rinv", n)))
                ts(probs[0:qn, n % 2, 0:nk], probs[0:qn, n % 2, 0:nk], st[:, 3:4], None, ALU.mult, None, "dve_mix",
                   (l, "p", n))

            def row_max(n):
                hd, i = items[n]
                q0, qn = TILES[i]
                nk = q0 + qn
                dve.wait_ge(*at((l, "s", n)))
                b = 2 + 2 * (n % 3)
                diag = flat(b, 256 + q0, qn)[0:qn]
                tt(diag, diag, neg_qk[0:qn, 0:qn], ALU.add, "dve_mix", (l, "masked", n))
                dve.wait_ge(*at((l, "masked", n)))
                if n >= 3:
                    dve.wait_ge(*at((l, "p", n - 3)))
                st = stat[0:qn, n % 3]
                nc.vector.reduce_max(st[:, 0:1], flat(b, 256, nk)[0:qn], AX)\
                    .then_inc(*mark("dve_mix", (l, "max", n)))
                dve.wait_ge(*at((l, "max", n)))
                ts(st[:, 1:2], st[:, 0:1], -SC, None, ALU.mult, None, "dve_mix", (l, "nmax", n))

            row_max(0)
            row_max(1)
            for n in range(len(items)):
                normalise(n)
                if n + 2 < len(items):
                    row_max(n + 2)
            split_lo(1)

            dve.wait_ge(*at((l, "br", 1)))
            nc.vector.memset(u_pad[:, :, 0:CV_W - 1], 0.0).then_inc(*mark("dve_mix", (l, "u_pad")))
            dve.wait_ge(*at((l, "u_pad")))
            for two in ((0, 1), (2, 3)):
                for w in range(CV_W):
                    for i in two:
                        src = u_pad[:, i, w:w + T]
                        label = (l, "cv_o", i) if w == CV_W - 1 else (l, "cvw", w, i)
                        if w == 0:
                            dve.wait_ge(*at((l, "glu", i)))
                            ts(cv_o[:, i, :], src, vcol("cvw", CV_W * i), vcol("cvb", i), ALU.mult, ALU.add,
                               "dve_mix", label)
                        else:
                            dve.wait_ge(*at((l, "cvw", w - 1, i)))
                            stt(cv_o[:, i, :], src, vcol("cvw", CV_W * i + w), cv_o[:, i, :], ALU.mult, ALU.add,
                                "dve_mix", label)
            dve.wait_ge(*at((l, "cv_mu")))
            for i in range(4):
                dve.wait_ge(*at((l, "cv_o", i)))
                tt(cv_o[:, i, :], cv_o[:, i, :], gate_s[:, 0, :], ALU.subtract, "dve_mix", (l, "cv_c", i))
            for m in range(4):
                merge(1, m)
            dve.wait_ge(*at((l, "cv_rt")))
            nc.vector.reciprocal(gate_s[:, 1, :], gate_s[:, 1, :]).then_inc(*mark("dve_mix", (l, "cv_r")))
            dve.wait_ge(*at((l, "cv_r")))
            for i in range(4):
                stt(cv_o[:, i, :], cv_o[:, i, :], vcol("cvg", i), gate_s[:, 1, :], ALU.mult, ALU.mult, "dve_mix",
                    (l, "cv_n", i))
                merge(1, 4 + i)
            split_lo(2)
            for m in range(KD):
                merge(2, m)
                if m:
                    dve.wait_ge(*at((l, "m_hi", m - 1)))
                    remainder(m_lo[:, m - 1, :], acc[:, m - 1, :], m_hi[:, m - 1, :], "dve_mix", (l, "m", m - 1))
            dve.wait_ge(*at((l, "m_hi", KD - 1)))
            remainder(m_lo[:, KD - 1, :], acc[:, KD - 1, :], m_hi[:, KD - 1, :], "dve_mix", (l, "m", KD - 1))
            for m in range(KD):
                t = TILE0["mix"] + m
                dve.wait_ge(*at((l, "tile", t)))
                dve.wait_ge(*at((l, "m", m)))
                stt(halves(acc[:, m, :]), halves(h_hi[:, m, :].bitcast(F32)), ALPHA, pair(tile0(l) + t), ALU.mult,
                    ALU.add, "dve_mix", (l, "evac", t))
                dve.wait_ge(*at((l, "evac", t)))
                stt(acc[:, m, :], h_lo[:, m, :].bitcast(F32), ALPHA, acc[:, m, :], ALU.mult, ALU.add, "dve_ln",
                    (l, "ln1", "x", m))

            def norm(which, ready):
                dve.wait_ge(*at((l, which, "mu")))
                if which == "ln1":
                    dve.wait_ge(*at((l, "ln1", "x", KD - 1)))
                for k in range(KD):
                    tt(acc[:, k, :], acc[:, k, :], gate_s[:, 0, :], ALU.subtract, "dve_ln", (l, which, "c", k))
                dve.wait_ge(*at((l, which, "rt")))
                nc.vector.reciprocal(gate_s[:, 1, :], gate_s[:, 1, :]).then_inc(*mark("dve_ln", (l, which, "r")))
                dve.wait_ge(*at((l, which, "r")))
                last = which == "ln2" and l == DEPTH - 1
                for k in range(KD + 2):
                    if k < KD:
                        stt(acc[:, k, :], acc[:, k, :], vcol(which + "g", k), gate_s[:, 1, :], ALU.mult, ALU.mult,
                            "dve_ln", (l, which, "n", k))
                    if k >= 2 and not last:
                        j = k - 2
                        dve.wait_ge(*at((l, which, "hi", j)))
                        stt(h_lo[:, j, :], acc[:, j, :], vcol(which + "b", j), h_hi[:, j, :].bitcast(F32), ALU.add,
                            ALU.subtract, "dve_ln", (*ready, j))

            norm("ln1", (l, "h_mid"))

            t0 = (l + 1) * MIX_TILES + EXP0[l] * PER_EXPERT
            g0 = (l + 1) * MIX_PANELS + EXP0[l] * PER_EXPERT
            def tok_remainder(n):
                dve.wait_ge(*at(("tok_hi", n)))
                part = slice(512 * (n % 2), 512 * (n % 2) + 512)
                tt(tok_lo[:, n // 2, part], psum[:, n % 4, :], tok_hi[:, n // 2, part].bitcast(F32), ALU.subtract,
                   "rt_dve", ("tok_lo", n))

            if l == 1:
                dve.wait_ge(*at((l, "logits")))
                for c in range(NT):
                    nc.vector.max(top_v[:, c, :], logits[:, c, :]).then_inc(*mark("rt_dve", (l, "top", c)))
                    dve.wait_ge(*at((l, "top", c)))
                    nc.vector.max_index(top_i[:, c, :], top_v[:, c, :], logits[:, c, :])\
                        .then_inc(*mark("rt_dve", (l, "top_i", c)))
                dve.wait_ge(*at((l, "top_i", NT - 1)))
                nc.vector.tensor_copy(top_f[:], top_i[:, :, 0:2]).then_inc(*mark("rt_dve", (l, "top_f")))
                tt(top_w[:, :, 1:2], top_v[:, :, 1:2], top_v[:, :, 0:1], ALU.subtract, "rt_dve", (l, "w_arg"))
                dve.wait_ge(*at((l, "w_exp")))
                ts(top_v[:, :, 0:1], top_w[:, :, 1:2], 1.0, None, ALU.add, None, "rt_dve", (l, "w_sum"))
                dve.wait_ge(*at((l, "w_sum")))
                nc.vector.reciprocal(top_w[:, :, 0:1], top_v[:, :, 0:1]).then_inc(*mark("rt_dve", (l, "w0")))
                dve.wait_ge(*at((l, "w0")))
                tt(top_w[:, :, 1:2], top_w[:, :, 1:2], top_w[:, :, 0:1], ALU.mult, "rt_dve", (l, "w1"))
                dve.wait_ge(*at((l, "w1")))
                for j, dst in ((0, gates), (1, g_sel)):
                    tt(dst[:], bc(expert_no[:], 1, NT), bc(top_f[:, :, j], 2, N_EXP), ALU.is_equal, "rt_dve",
                       (l, "one_hot", j))
                    dve.wait_ge(*at((l, "one_hot", j)))
                    if j == 0:
                        nc.vector.tensor_copy(chosen[:], gates[:]).then_inc(*mark("rt_dve", "chosen0"))
                    else:
                        dve.wait_ge(*at("chosen0"))
                        tt(chosen[:], chosen[:], g_sel[:], ALU.add, "rt_dve", "chosen")
                        dve.wait_ge(*at("chosen"))
                    tt(dst[:], dst[:], bc(top_w[:, :, j], 2, N_EXP), ALU.mult, "rt_dve", (l, "weighted", j))
                    dve.wait_ge(*at((l, "weighted", j)))
                tt(gates[:], gates[:], g_sel[:], ALU.add, "rt_dve", (l, "gates"))
                dve.wait_ge(*at((l, "gates")))
                for n in range(4):
                    tok_remainder(n)
                dve.wait_ge(*at("columns"))
                cols4 = psum[:, 5, 0:32].rearrange("p (a b) -> p a b", b=N_EXP)
                tt(slots[:, :, 0:N_EXP], cols4, chosen[:, 1:NT, :], ALU.mult, "rt_dve", "slots")
                nc.vector.reduce_max(load_max[:, 0:1], psum[:, 5, 32:40], AX).then_inc(*mark("rt_dve", "load"))
                dve.wait_ge(*at("load"))
                ts(slots[:, :, 0:N_EXP], slots[:, :, 0:N_EXP], -1.0, None, ALU.add, None, "rt_dve", "slots1")
                dve.wait_ge(*at("slots1"))
                ts(slots[:, :, N_EXP:], slots[:, :, 0:1], float(-CAP), None, ALU.add, None, "rt_dve", "slots2")
                ts(load_max[:, 1:2], load_max[:, 0:1], float(CAP), 1.0, ALU.is_gt, ALU.add, "rt_dve", "over1")
                ts(load_max[:, 2:3], load_max[:, 0:1], float(2 * CAP), None, ALU.is_gt, None, "rt_dve", "over2")
                dve.wait_ge(*at("over2"))
                tt(rounds_i[:], load_max[:, 1:2], load_max[:, 2:3], ALU.add, "rt_dve", "rounds")
                for n in range(4, 8):
                    tok_remainder(n)

            def low(n, before):
                cols = WIDE if n % PER_EXPERT < 2 * F_TILES else DEEP
                dve.wait_ge(hi_done, before + (g0 + n + 1))
                nc.vector.tensor_tensor(ffn_w(l, n, 1)[:, 0:cols], raw[:, n % RAW, 0:cols],
                                        ffn_w(l, n, 0)[:, 0:cols].bitcast(F32), ALU.subtract).then_inc(lo_done[1], 1)

            if l == 0:
                dve.wait_ge(lo_done[0], g0 // 2)
                dve.wait_ge(lo_done[1], g0 // 2)
                low(1, 0)
                low(3, 0)
                for m in range(KD):
                    ts(acc[:, m, :], acc[:, m, :], vcol("ln1b", m), ALPHA, ALU.add, ALU.mult, "y_init", (l, "y0", m))
                for e in range(EXPERTS[0]):
                    for f in range(F_TILES):
                        n = e * PER_EXPERT + 2 * f
                        cnt = e * F_TILES + f
                        dve.wait_ge(silu_done, cnt + 3)
                        dve.wait_ge(tile_done, t0 + n + 2)
                        if cnt >= 2:
                            dve.wait_ge(actl_done, cnt - 1)
                        nc.vector.tensor_tensor(halves(act_f[:, f % 2, :]), (pair, work2)[f % 2](1), halves(gate_s[:, f % 2, :]),
                                                ALU.mult).then_inc(act_done, 1)
                        dve.wait_ge(acth_done, cnt + 1)
                        nc.vector.tensor_tensor(act_lo[:, f, :], act_f[:, f % 2, :], act_hi[:, f, :].bitcast(F32),
                                                ALU.subtract).then_inc(actl_done, 1)
                        low(n + 5, 0)
                    for m in range(KD):
                        n = e * PER_EXPERT + 2 * F_TILES + m
                        dve.wait_ge(tile_done, t0 + n + 1)
                        nc.vector.tensor_tensor(halves(acc[:, m, :]), halves(acc[:, m, :]), pair(n), ALU.add)\
                            .then_inc(y_done, 1)
                        if m % 2 == 1 and n + AHEAD < 2 * PER_EXPERT:
                            low(n + AHEAD, 0)
                dve.wait_ge(y_done, 1 + EXPERTS[0] * KD)
                norm("ln2", (l + 1, "h"))
                continue

            def make_pick(e1, slot):
                nc.vector.tensor_tensor(pick[:, slot], bc(column_no[:], 1, 4),
                                        slots[:, :, e1].broadcast_to([P, 4, CAP]), ALU.is_equal).then_inc(m_pick, 1)

            def copy_x(v1):
                for m in range(KD):
                    dve.wait_ge(m_gather, v1 * KD + m + 2)
                    nc.vector.tensor_copy(xc[:, m].rearrange("p a n -> p (a n)"), psum[:, 6 + m % 2, 0:2 * CAP])\
                        .then_inc(m_x, 1)

            def add_y(v):
                for m in range(KD):
                    dve.wait_ge(m_scat, v * KD + m + 2)
                    nc.vector.tensor_tensor(acc[:, m, N_META:T], acc[:, m, N_META:T], psum[:, 4 + m % 2, :],
                                            ALU.add).then_inc(m_add, 1)

            def add_parts(dst, b):
                both = psum[:, b, 0:2 * CAP].rearrange("p (a n) -> p n a", a=2)
                return nc.vector.reduce_sum(dst, both, AX)

            nc.vector.memset(yt_hi.bitcast(F32), 0.0).then_inc(*mark("rt_dve", "z0"))
            nc.vector.memset(yt_lo.bitcast(F32), 0.0).then_inc(*mark("rt_dve", "z1"))
            nc.vector.memset(put[:].bitcast(F32), 0.0).then_inc(*mark("rt_dve", "z2"))
            dve.wait_ge(*at("z2"))
            dve.wait_ge(const_in, 160)
            make_pick(bass.ds(0, 1), 0)
            rounds = rounds_of(dve)
            dve.wait_ge(lo_done[0], g0 // 2)
            dve.wait_ge(lo_done[1], g0 // 2)
            low(1, 0)
            low(3, 0)
            copy_x(0)
            dve.wait_ge(*at(("scaled", KD - 1)))
            with nc.vector.Fori(0, rounds) as r:
                with nc.vector.Fori(0, N_EXP // 2) as i:
                    before = r * (N_EXP * PER_EXPERT) + i * (2 * PER_EXPERT)
                    for x in range(2):
                        v = r * N_EXP + i * 2 + x
                        dve.wait_ge(m_gather, v * KD + KD + 1)
                        make_pick(bass.ds(i * 2 + (x + 1), 1), 1 - x)
                        for f in range(F_TILES):
                            n = x * PER_EXPERT + 2 * f
                            b = 2 * (f % 2)
                            dve.wait_ge(tile_done, before + (t0 + n + 1))
                            dve.wait_ge(m_act, v * F_TILES + (f + 1))
                            add_parts(moe_g[:, f % 2, :], b).then_inc(m_gsum, 1)
                            dve.wait_ge(tile_done, before + (t0 + n + 2))
                            dve.wait_ge(ma_l, v * F_TILES + max(f, 1))
                            add_parts(moe_a[:, f % 2, :], b + 1).then_inc(m_usum, 1)
                            dve.wait_ge(m_silu, v * F_TILES + (f + 2))
                            dve.wait_ge(m_usum, v * F_TILES + (f + 3))
                            nc.vector.tensor_tensor(moe_a[:, f % 2, :], moe_a[:, f % 2, :], moe_g[:, f % 2, :],
                                                    ALU.mult).then_inc(m_act, 1)
                            dve.wait_ge(ma_h, v * F_TILES + f + 2)
                            nc.vector.tensor_tensor(ma[:, f, 1, :], moe_a[:, f % 2, :], ma[:, f, 0, :].bitcast(F32),
                                                    ALU.subtract).then_inc(ma_l, 1)
                            if f < F_TILES - 1:
                                low(n + 5, before)
                        add_y(v)
                        low(x * PER_EXPERT + 2 * F_TILES + 3, before)
                        copy_x(v + 1)
                        for m in range(KD):
                            n = x * PER_EXPERT + 2 * F_TILES + m
                            dve.wait_ge(tile_done, before + (t0 + n + 1))
                            dve.wait_ge(m_yt, v * KD + max(m, 1))
                            add_parts(y_f[:, m % 2, :], m % 2).then_inc(m_y, 1)
                            if m % 2 == 1:
                                low(n + AHEAD, before)
                            if m % 4 == 3:
                                half = slice(512 * (m // 4), 512 * (m // 4) + 512)
                                for ct in range(2):
                                    dve.wait_ge(m_yhi, v * 4 + (2 * (m // 4) + ct + 2))
                                    nc.vector.scalar_tensor_tensor(
                                        out=yt_lo[:, ct, half], in0=psum[0:CT, 2 + ct, :], scalar=gate_c[:, ct:ct + 1],
                                        in1=yt_hi[:, ct, half].bitcast(F32), op0=ALU.mult, op1=ALU.subtract)\
                                        .then_inc(m_ylo, 1)
                dve.wait_ge(m_pick, r * N_EXP + (N_EXP + 2))
                nc.vector.tensor_scalar(slots[:], slots[:], float(CAP), None, ALU.subtract).then_inc(m_shift, 1)
                dve.wait_ge(m_shift, r + 1)
            add_y(rounds * N_EXP)
            dve.wait_ge(m_add, rounds * (N_EXP * KD) + (KD + 1))
            norm("ln2", None)


def blocks(w, cols):
    w = w[:, cols]
    return np.ascontiguousarray(w.reshape(-1, P, len(cols)).transpose(1, 0, 2)).reshape(P, -1)


def mixer_panels(w_in, w_uq, w_ukv, w_br, w_out):
    sizes = (256, 128, 32, 1536, 512, 4, 4, 512, 512, D, D, D)
    cq, ckv, kr, dn, z, b, _, cva, cvb, *gate = np.concatenate([[0], np.cumsum(sizes)])[:-1].tolist()
    tile = lambda c0, i: np.arange(c0 + P * i, c0 + P * (i + 1))
    out = [blocks(w_in, tile(dn, i)) for i in range(12)]
    small = np.zeros((P, WIDE), w_in.dtype)
    small[:, 0:8 * KD] = blocks(w_in, np.arange(b, b + 8))
    out.append(small)
    def gates(n):
        return [blocks(w_in, tile(gate[(1, 0, 2)[n]], i)) for i in range(KD)]

    def branch(n):
        return [np.concatenate([blocks(w_br[n], tile(0, 2 * i + j)) for j in range(2)], 1) for i in range(KD // 2)]

    out += gates(0)
    out += [blocks(w_in, tile(z, i)) for i in range(4)]
    out += [blocks(w_in, tile(cq, i)) for i in range(2)] + [blocks(w_in, tile(ckv, 0))]
    turned = np.concatenate([np.arange(ROPE // 2, ROPE), np.arange(ROPE // 2)])
    out.append(blocks(w_in, np.concatenate([np.arange(kr - NOPE, kr + ROPE), kr + turned])))
    out += branch(0)
    for half in range(2):
        out.append(np.concatenate([blocks(w_uq, np.concatenate([np.arange(QK * hd, QK * (hd + 1)),
                                                               QK * hd + NOPE + turned]))
                                   for hd in range(4 * half, 4 * half + 4)], 1))
    part = lambda hd, c0: np.arange(hd * (NOPE + VD) + c0, hd * (NOPE + VD) + c0 + 64)
    out.append(np.concatenate([blocks(w_ukv, np.concatenate([part(2 * i, c0), part(2 * i + 1, c0)]))
                               for c0 in (0, NOPE) for i in range(4)], 1))
    for i in range(4):
        out += [blocks(w_in, tile(cva, i)), blocks(w_in, tile(cvb, i))]
    out += gates(1) + gates(2) + branch(1) + branch(2)
    out += [blocks(w_out, tile(0, i)) for i in range(8)]
    assert len(out) == MIX_PANELS
    return np.stack(out)


def columns(x):
    return x.reshape(-1, P).T


def host_arrays(a):
    f = np.float32
    got = {}
    h0 = np.concatenate([a["meta_tokens"], a["x"][0]], 0)
    got["h0"] = np.ascontiguousarray(h0.T.reshape(KD, P, T).transpose(1, 0, 2))
    got["mix_panels"] = np.stack([
        mixer_panels(a["w_in"][l], a["mla_w_uq"][l], a["mla_w_ukv"][l],
                     (a["w_br_dn"][l], a["w_br_mla"][l], a["w_br_cv"][l]), a["w_mix_out"][l]) for l in range(DEPTH)])
    FE = F_TILES * P
    experts = [tuple(w[0][:, x * FE:(x + 1) * FE] for w in (a["ffn_w_gate"], a["ffn_w_up"]))
               + (a["ffn_w_down"][0][x * FE:(x + 1) * FE],) for x in range(EXPERTS[0])]
    experts += [tuple(w[0][e] for w in (a["moe_w_gate"], a["moe_w_up"], a["moe_w_down"])) for e in range(N_EXP)]
    ups = experts + [experts[EXPERTS[0]]]
    tile = lambda i: np.arange(P * i, P * (i + 1))
    got["up_panels"] = np.stack([np.stack([blocks(w, tile(i)) for i in range(F_TILES) for w in (wg, wu)])
                                 for wg, wu, _ in ups])
    got["down_panels"] = np.stack([np.stack([blocks(wd, tile(i)) for i in range(KD)]) for _, _, wd in experts])
    vecs = []
    for l in range(DEPTH):
        conv = a["dn_conv_w"][l].reshape(4, 12, P).transpose(2, 1, 0).reshape(P, -1)
        cvw = a["cv_dw_w"][l].reshape(CV_W, 4, P).transpose(2, 1, 0).reshape(P, -1)
        row = lambda x: np.broadcast_to(x[None, :], (P, x.shape[0]))
        vecs.append(np.concatenate([
            columns(a["mla_q_norm"][l]), columns(a["mla_kv_norm"][l]), conv, columns(a["dn_o_norm"][l]), cvw,
            columns(a["cv_dw_b"][l]), columns(a["cv_ln_g"][l]), columns(a["cv_ln_b"][l]), columns(a["ln1_g"][l]),
            columns(a["ln1_b"][l]), columns(a["ln2_g"][l]), columns(a["ln2_b"][l]), row(a["dn_a_log"][l]),
            row(a["dn_dt_bias"][l])], 1))
    got["vec"] = np.stack(vecs)
    got["router"] = blocks(a["moe_w_router"][0], np.arange(N_EXP)).reshape(P, KD, N_EXP)
    i, j = np.arange(P)[None, :], np.arange(P)[:, None]
    got["ident"] = (i == j).astype(f)
    got["cum_mask"] = (j <= i).astype(f)
    got["neg_ji"] = np.where(i < j, f(NEG), f(0))
    got["neg_qk"] = np.where(i > j, f(NEG), f(0))
    got["level_mask"] = np.stack([((j >> b) % 2 == 1) & ((i >> b) == (j >> b) - 1) for b in range(LEVELS)], 1)\
        .astype(f)
    meta = np.ones((P, NT, DN_H), f)
    meta[N_META:, 0, :] = 0
    got["meta_rows"] = meta
    inv = f(10000.0) ** (-np.arange(0, ROPE, 2, dtype=f) / f(ROPE))
    ang = (np.arange(T, dtype=f)[:, None] * inv[None, :]).T
    rope = np.zeros((P, T), f)
    rope[NOPE:QK] = np.concatenate([np.cos(ang), np.cos(ang)])
    rope[QK:P] = np.concatenate([-np.sin(ang), np.sin(ang)])
    got["rope"] = rope
    got["expert_no"] = np.broadcast_to(np.arange(N_EXP, dtype=f)[None, :], (P, N_EXP))
    got["column_no"] = np.broadcast_to(np.arange(CAP, dtype=f)[None, :], (P, CAP))
    return {f"in_{k}": np.ascontiguousarray(v) for k, v in got.items()}


def kernel(**inputs):
    import concourse.bacc as bacc
    from concourse.bass_utils import run_bass_kernel_spmd

    arrays = host_arrays({k: np.asarray(x) for k, x in inputs.items()})
    notes = None
    for _ in range(2):
        nc = bacc.Bacc("TRN2", target_bir_lowering=False, num_devices=1)
        ins = {k[3:]: nc.dram_tensor(k, x.shape, mybir.dt.from_np(x.dtype), kind="ExternalInput").ap()
               for k, x in arrays.items()}
        out = nc.dram_tensor("out", (P, KD, SEQ), F32, kind="ExternalOutput").ap()
        counts = Counts(notes)
        program(nc, counts, ins, out)
        notes = counts.notes
    r = run_bass_kernel_spmd(nc, [arrays], core_ids=[0])
    got = r.results[0]["out"]
    return np.ascontiguousarray(got.transpose(1, 0, 2)).reshape(D, SEQ).T[None]
```
